# Optimizing a Trainium2 kernel written in Bass

```python
import math
import jax, jax.numpy as jnp
from jax import lax
import numpy as np

D_MODEL = 1024
BATCH = 1
SEQ = 256
DEPTH = 2
DEC_BATCH = 8
DEC_SEQ = 8
PAST_LEN = 2048
PAGE_SIZE = 128

N_EVEN = (DEPTH + 1) // 2
N_ODD = DEPTH // 2
D_POOL = D_MODEL // 2
POOL_WINDOWS = (2, 4, 8, 16)
N_POOL_GROUPS = len(POOL_WINDOWS)
POOL_GROUP = D_POOL // N_POOL_GROUPS
POOL_BUF = max(POOL_WINDOWS) - 1
D_RNN = D_MODEL // 2
RNN_HEADS = 8
RNN_HEAD_DIM = D_RNN // RNN_HEADS
RNN_CONV = 4
RG_C = 8.0
D_IN_EVEN = D_POOL + 2 * D_RNN
D_CONV = D_MODEL
CONV_WIDTH = 31
PEER_HEADS = 8
PEER_NKEYS = 128
PEER_N = PEER_NKEYS * PEER_NKEYS
PEER_DQ = 256
PEER_DH = PEER_DQ // 2
PEER_TOPK = 16
PEER_BLOCK = 128
LN_EPS = 1e-5
ALPHA = (2.0 * DEPTH) ** 0.25
BETA = (8.0 * DEPTH) ** -0.25

kernel_name = 'hybrid_pool_rglru_conformer_peer_step'

def _layer_norm(x, g, b):
    xf = x.astype(jnp.float32)
    mu = jnp.mean(xf, axis=-1, keepdims=True)
    var = jnp.mean(jnp.square(xf - mu), axis=-1, keepdims=True)
    y = (xf - mu) * lax.rsqrt(var + LN_EPS) * g.astype(jnp.float32) + b.astype(jnp.float32)
    return y.astype(x.dtype)

def _causal_dwconv(x_ext, w, b):
    c = x_ext.shape[-1]
    y = lax.conv_general_dilated(x_ext, w[:, None, :].astype(x_ext.dtype), (1,), 'VALID',
                                 dimension_numbers=('NWC', 'WIO', 'NWC'), feature_group_count=c)
    return y + b.astype(x_ext.dtype)

def _multiscale_pool(xa_ext, start):
    bsz, length, _ = xa_ext.shape
    s = length - POOL_BUF
    xg = xa_ext.astype(jnp.float32).reshape(bsz, length, N_POOL_GROUPS, POOL_GROUP)
    csum = jnp.concatenate([jnp.zeros_like(xg[:, :1]), jnp.cumsum(xg, axis=1)], axis=1)
    pos = start + jnp.arange(s)
    means = []
    for g, w in enumerate(POOL_WINDOWS):
        win = csum[:, POOL_BUF + 1:POOL_BUF + 1 + s, g] - csum[:, POOL_BUF + 1 - w:POOL_BUF + 1 - w + s, g]
        cnt = jnp.minimum(pos + 1, w).astype(jnp.float32)
        means.append(win / cnt[None, :, None])
    mean = jnp.stack(means, axis=2)
    return (mean - xg[:, POOL_BUF:]).astype(xa_ext.dtype)

def _rglru(xc, h0, wa, ba, wx, bx, lam):
    bsz, s, c = xc.shape
    xf = xc.astype(jnp.float32)
    xh = xf.reshape(bsz, s, RNN_HEADS, RNN_HEAD_DIM)
    r = jax.nn.sigmoid(jnp.einsum('bshi,hij->bshj', xh, wa.astype(jnp.float32)).reshape(bsz, s, c) + ba.astype(jnp.float32))
    i = jax.nn.sigmoid(jnp.einsum('bshi,hij->bshj', xh, wx.astype(jnp.float32)).reshape(bsz, s, c) + bx.astype(jnp.float32))
    log_a = -RG_C * r * jax.nn.softplus(-lam.astype(jnp.float32))
    a = jnp.exp(log_a)
    u = jnp.sqrt(-jnp.expm1(2.0 * log_a)) * (i * xf)
    u = u.at[:, 0].add(a[:, 0] * h0.astype(jnp.float32))

    def combine(p, q):
        return p[0] * q[0], q[0] * p[1] + q[1]

    _, h = lax.associative_scan(combine, (a, u), axis=1)
    h = h.astype(xc.dtype)
    return h, h[:, -1]

def _even_mixer(x, pool_buf, conv_buf, h0, start, w_in, pool_w, pool_scale, conv_w, conv_b, wa, ba, wx, bx, lam, w_out):
    bsz, s, _ = x.shape
    z = x @ w_in
    xa = z[..., :D_POOL]
    xb = z[..., D_POOL:D_POOL + D_RNN]
    xg = z[..., D_POOL + D_RNN:]
    xa_ext = jnp.concatenate([pool_buf.astype(xa.dtype), xa], axis=1)
    pooled = _multiscale_pool(xa_ext, start)
    ya = jnp.einsum('bsgc,gcd->bsgd', pooled, pool_w).reshape(bsz, s, D_POOL) * pool_scale
    xb_ext = jnp.concatenate([conv_buf.astype(xb.dtype), xb], axis=1)
    xc = _causal_dwconv(xb_ext, conv_w, conv_b)
    h, h_last = _rglru(xc, h0, wa, ba, wx, bx, lam)
    yb = h * jax.nn.gelu(xg)
    out = jnp.concatenate([ya, yb], axis=-1) @ w_out
    return out, xa_ext[:, -POOL_BUF:], xb_ext[:, -(RNN_CONV - 1):], h_last

def _odd_mixer(x, conv_buf, w_glu, dw_w, dw_b, ln_g, ln_b, w_pw):
    z = x @ w_glu
    g = z[..., :D_CONV] * jax.nn.sigmoid(z[..., D_CONV:])
    g_ext = jnp.concatenate([conv_buf.astype(g.dtype), g], axis=1)
    c = _causal_dwconv(g_ext, dw_w, dw_b)
    c = jax.nn.silu(_layer_norm(c, ln_g, ln_b))
    return c @ w_pw, g_ext[:, -(CONV_WIDTH - 1):]

def _peer_block(xb, wq, k1, k2, u, v):
    n = xb.shape[0]
    q = (xb @ wq).reshape(n, PEER_HEADS, PEER_DQ).astype(jnp.float32)
    s1 = jnp.einsum('nhd,kd->nhk', q[..., :PEER_DH], k1.astype(jnp.float32))
    s2 = jnp.einsum('nhd,kd->nhk', q[..., PEER_DH:], k2.astype(jnp.float32))
    v1, i1 = lax.top_k(s1, PEER_TOPK)
    v2, i2 = lax.top_k(s2, PEER_TOPK)
    cand = (v1[..., :, None] + v2[..., None, :]).reshape(n, PEER_HEADS, PEER_TOPK * PEER_TOPK)
    sv, ci = lax.top_k(cand, PEER_TOPK)
    e = (jnp.take_along_axis(i1, ci // PEER_TOPK, axis=-1) * PEER_NKEYS
         + jnp.take_along_axis(i2, ci % PEER_TOPK, axis=-1))
    gate = jax.nn.softmax(sv, axis=-1)
    act = jax.nn.gelu(jnp.einsum('nhkd,nd->nhk', u[e], xb).astype(jnp.float32))
    wgt = (gate * act).astype(xb.dtype)
    return jnp.einsum('nhk,nhkd->nd', wgt, v[e])

def _peer(x, wq, k1, k2, u, v):
    bsz, s, d = x.shape
    t = bsz * s
    nb = -(-t // PEER_BLOCK)
    xt = jnp.pad(x.reshape(t, d), ((0, nb * PEER_BLOCK - t), (0, 0))).reshape(nb, PEER_BLOCK, d)
    y = lax.map(lambda xb: _peer_block(xb, wq, k1, k2, u, v), xt)
    return y.reshape(nb * PEER_BLOCK, d)[:t].reshape(bsz, s, d)

def _trunk(x, st_pool, st_rconv, st_h, st_conv, start, p):
    pools, rconvs, hs, convs = [], [], [], []
    for layer in range(DEPTH):
        j = layer // 2
        if layer % 2 == 0:
            m, pb, rb, hl = _even_mixer(x, st_pool[j], st_rconv[j], st_h[j], start,
                                        p['w_in_even'][j], p['pool_w'][j], p['pool_scale'][j],
                                        p['rnn_conv_w'][j], p['rnn_conv_b'][j], p['rg_wa'][j], p['rg_ba'][j],
                                        p['rg_wx'][j], p['rg_bx'][j], p['rg_lambda'][j], p['w_out_even'][j])
            pools.append(pb)
            rconvs.append(rb)
            hs.append(hl)
        else:
            m, cb = _odd_mixer(x, st_conv[j], p['w_glu'][j], p['dw_w'][j], p['dw_b'][j],
                               p['conv_ln_g'][j], p['conv_ln_b'][j], p['w_pw'][j])
            convs.append(cb)
        x = _layer_norm(ALPHA * x + m, p['ln_mix_g'][layer], p['ln_mix_b'][layer])
        f = _peer(x, p['peer_wq'][layer], p['peer_k1'][layer], p['peer_k2'][layer],
                  p['peer_u'][layer], p['peer_v'][layer])
        x = _layer_norm(ALPHA * x + f, p['ln_ffn_g'][layer], p['ln_ffn_b'][layer])
    return x, jnp.stack(pools), jnp.stack(rconvs), jnp.stack(hs), jnp.stack(convs)

def setup_inputs(seed: int = 0) -> dict:
    key = jax.random.key(seed)
    ks = jax.random.split(key, 40)
    f32 = jnp.float32

    def nrm(k, shape, scale):
        return jax.random.normal(k, shape, f32) * scale

    def gain(k, shape):
        return 1.0 + 0.05 * jax.random.normal(k, shape, f32)

    a_init = jax.random.uniform(ks[15], (N_EVEN, D_RNN), f32, 0.9, 0.999)
    s_init = a_init ** (1.0 / RG_C)
    return {
        'x_prompt': nrm(ks[0], (BATCH, SEQ, D_MODEL), 1.0),
        'x_sample': nrm(ks[1], (DEC_BATCH, DEC_SEQ, D_MODEL), 1.0),
        'state_pool': nrm(ks[2], (N_EVEN, DEC_BATCH, POOL_BUF, D_POOL), 1.0),
        'state_rnn_conv': nrm(ks[3], (N_EVEN, DEC_BATCH, RNN_CONV - 1, D_RNN), 1.0),
        'state_rnn_h': nrm(ks[4], (N_EVEN, DEC_BATCH, D_RNN), 0.5),
        'state_conv': nrm(ks[5], (N_ODD, DEC_BATCH, CONV_WIDTH - 1, D_CONV), 1.0),
        'w_in_even': nrm(ks[6], (N_EVEN, D_MODEL, D_IN_EVEN), D_MODEL ** -0.5),
        'pool_w': nrm(ks[7], (N_EVEN, N_POOL_GROUPS, POOL_GROUP, POOL_GROUP), POOL_GROUP ** -0.5),
        'pool_scale': gain(ks[8], (N_EVEN, D_POOL)),
        'rnn_conv_w': nrm(ks[9], (N_EVEN, RNN_CONV, D_RNN), RNN_CONV ** -0.5),
        'rnn_conv_b': nrm(ks[10], (N_EVEN, D_RNN), 0.02),
        'rg_wa': nrm(ks[11], (N_EVEN, RNN_HEADS, RNN_HEAD_DIM, RNN_HEAD_DIM), RNN_HEAD_DIM ** -0.5),
        'rg_ba': nrm(ks[12], (N_EVEN, D_RNN), 0.02),
        'rg_wx': nrm(ks[13], (N_EVEN, RNN_HEADS, RNN_HEAD_DIM, RNN_HEAD_DIM), RNN_HEAD_DIM ** -0.5),
        'rg_bx': nrm(ks[14], (N_EVEN, D_RNN), 0.02),
        'rg_lambda': jnp.log(s_init) - jnp.log1p(-s_init),
        'w_out_even': nrm(ks[16], (N_EVEN, D_POOL + D_RNN, D_MODEL), BETA * (D_POOL + D_RNN) ** -0.5),
        'w_glu': nrm(ks[17], (N_ODD, D_MODEL, 2 * D_CONV), D_MODEL ** -0.5),
        'dw_w': nrm(ks[18], (N_ODD, CONV_WIDTH, D_CONV), CONV_WIDTH ** -0.5),
        'dw_b': nrm(ks[19], (N_ODD, D_CONV), 0.02),
        'conv_ln_g': gain(ks[20], (N_ODD, D_CONV)),
        'conv_ln_b': nrm(ks[21], (N_ODD, D_CONV), 0.02),
        'w_pw': nrm(ks[22], (N_ODD, D_CONV, D_MODEL), BETA * D_CONV ** -0.5),
        'peer_wq': nrm(ks[23], (DEPTH, D_MODEL, PEER_HEADS * PEER_DQ), D_MODEL ** -0.5),
        'peer_k1': nrm(ks[24], (DEPTH, PEER_NKEYS, PEER_DH), PEER_DH ** -0.5),
        'peer_k2': nrm(ks[25], (DEPTH, PEER_NKEYS, PEER_DH), PEER_DH ** -0.5),
        'peer_u': nrm(ks[26], (DEPTH, PEER_N, D_MODEL), D_MODEL ** -0.5),
        'peer_v': nrm(ks[27], (DEPTH, PEER_N, D_MODEL), BETA),
        'ln_mix_g': gain(ks[28], (DEPTH, D_MODEL)),
        'ln_mix_b': nrm(ks[29], (DEPTH, D_MODEL), 0.02),
        'ln_ffn_g': gain(ks[30], (DEPTH, D_MODEL)),
        'ln_ffn_b': nrm(ks[31], (DEPTH, D_MODEL), 0.02),
    }

def reference(x_prompt, x_sample, state_pool, state_rnn_conv, state_rnn_h, state_conv,
              w_in_even, pool_w, pool_scale, rnn_conv_w, rnn_conv_b, rg_wa, rg_ba, rg_wx, rg_bx,
              rg_lambda, w_out_even, w_glu, dw_w, dw_b, conv_ln_g, conv_ln_b, w_pw,
              peer_wq, peer_k1, peer_k2, peer_u, peer_v, ln_mix_g, ln_mix_b, ln_ffn_g, ln_ffn_b):
    p = dict(w_in_even=w_in_even, pool_w=pool_w, pool_scale=pool_scale, rnn_conv_w=rnn_conv_w,
             rnn_conv_b=rnn_conv_b, rg_wa=rg_wa, rg_ba=rg_ba, rg_wx=rg_wx, rg_bx=rg_bx,
             rg_lambda=rg_lambda, w_out_even=w_out_even, w_glu=w_glu, dw_w=dw_w, dw_b=dw_b,
             conv_ln_g=conv_ln_g, conv_ln_b=conv_ln_b, w_pw=w_pw, peer_wq=peer_wq,
             peer_k1=peer_k1, peer_k2=peer_k2, peer_u=peer_u, peer_v=peer_v,
             ln_mix_g=ln_mix_g, ln_mix_b=ln_mix_b, ln_ffn_g=ln_ffn_g, ln_ffn_b=ln_ffn_b)
    bp = x_prompt.shape[0]
    dt = x_prompt.dtype
    y_prompt, pool_p, rconv_p, h_p, conv_p = _trunk(
        x_prompt,
        jnp.zeros((N_EVEN, bp, POOL_BUF, D_POOL), dt),
        jnp.zeros((N_EVEN, bp, RNN_CONV - 1, D_RNN), dt),
        jnp.zeros((N_EVEN, bp, D_RNN), dt),
        jnp.zeros((N_ODD, bp, CONV_WIDTH - 1, D_CONV), dt),
        0, p)
    y_sample, pool_s, rconv_s, h_s, conv_s = _trunk(
        x_sample, state_pool, state_rnn_conv, state_rnn_h, state_conv, PAST_LEN, p)
    return (y_prompt, y_sample, pool_p, rconv_p, h_p, conv_p, pool_s, rconv_s, h_s, conv_s)


_drawn_inputs = setup_inputs


def setup_inputs(seed=0):
    import zlib

    import numpy as np

    out = dict(_drawn_inputs(seed))
    spreads = {}
    factors = {'rg_ba': 6.374, 'rg_bx': 5.047, 'dw_b': 2.779, 'conv_ln_b': 4.201}
    for name, (base, spread) in spreads.items():
        noise = np.random.default_rng([zlib.crc32(name.encode()), seed]).standard_normal(out[name].shape)
        drawn = base * np.exp(spread * noise) if base else spread * noise
        out[name] = __import__('jax').numpy.asarray(drawn.astype(out[name].dtype))
    for name, factor in factors.items():
        out[name] = (out[name] * factor).astype(out[name].dtype)
    return out
```

```python
import concourse.bass as bass
from concourse import mybir
from contextlib import ExitStack
import numpy as np

F32 = mybir.dt.float32
I32 = mybir.dt.int32
U32 = mybir.dt.uint32
ALU = mybir.AluOpType
ACT = mybir.ActivationFunctionType
AX = mybir.AxisListType

P = 128
D = 1024
KD = D // P
SEQ, DB, DS = 256, 8, 8
NS = DB * DS
NT = SEQ + NS
HALF = D // 2
JR = HALF // P
PB, RB, CB = 15, 3, 30
CW = 31
HEADS, NK, TOPK = 8, 128, 16
NE = NK * NK
ALPHA = (2.0 * 2) ** 0.25
EPS = 1e-5
RING = 8
WSLOT = 2
V_CW, V_CB, V_BA, V_BX, V_LAM, V_PS, V_DB, V_CG, V_CBT, V_N = 0, 16, 20, 24, 28, 32, 36, 44, 52, 60
TILES = ((0, 8), (1, 8), (2, 4))


def psum_groups():
    g = [("vec",), ("dw", 0), ("dw", 1), ("key", 0), ("stp",), ("srh",)]
    for layer in range(2):
        g += [("xT", layer, 0, n, q) for n in range(3) for q in range(2)]
        if layer == 0:
            g += [("z0", ft) for ft in range(12)]
            g += [("pst", k) for k in range(4)]
            g += [("ya", j) for j in range(JR)]
            g += [(w, j) for j in range(JR) for w in ("ga", "gx")]
            g += [("hst", k) for k in range(2)]
        else:
            g += [("scv", p, q) for p in range(2) for q in range(2)]
            g += [("z1", c, i) for c in range(4) for i in range(4)]
            g += [("cst", k) for k in range(6)]
            g += [("mu",), ("var",)]
        g += [("o", layer, n, h) for n in range(3) for h in range(2)]
        g += [("xT", layer, 1, n, q) for n in range(3) for q in range(2)]
        g += [("q", layer, ft) for ft in range(16)]
        g += [("s", layer, n, i) for n, heads in TILES for i in range(heads // 2)]
        g += [("fold", layer, h) for h in range(2)]
    return g


GROUPS = psum_groups()
GID = {name: i for i, name in enumerate(GROUPS)}


def build(nc, x_prompt, x_sample, state_pool, state_rnn_conv, state_rnn_h, state_conv,
          w_in_even, pool_w, pool_scale, rnn_conv_w, rnn_conv_b, rg_wa, rg_ba, rg_wx, rg_bx,
          rg_lambda, w_out_even, w_glu, dw_w, dw_b, conv_ln_g, conv_ln_b, w_pw,
          peer_wq, peer_k1, peer_k2, peer_u, peer_v, ln_mix_g, ln_mix_b, ln_ffn_g, ln_ffn_b,
          y_prompt, y_sample, o_pool_p, o_rconv_p, o_h_p, o_conv_p, o_pool_s, o_rconv_s, o_h_s, o_conv_s):
    ctx = ExitStack()
    with ctx:
        def sb(name, shape, dt=F32, stack=ctx):
            return stack.enter_context(nc.sbuf_tensor(name, shape, dt))

        def sem(name):
            return ctx.enter_context(nc.semaphore(name))

        ident = sb("ident", [P, P])
        foldm = sb("foldm", [P, P])
        mean_m = sb("mean_m", [P, P])
        iota_i = sb("iota_i", [P, 16], I32)
        iota_f = sb("iota_f", [P, 16])
        inv_cnt = sb("inv_cnt", [P, JR, 16])
        vecs = sb("vecs", [P, V_N])
        taps = sb("taps", [P, CW * KD])
        spc = sb("spc", [P, JR])
        keyT = sb("keyT", [P, 4, P])
        poolw = sb("poolw", [P, JR, P])
        bda = sb("bda", [P, JR, P])
        bdx = sb("bdx", [P, JR, P])
        sm = sb("sm", [P, 64])
        x = sb("x", [P, 3, D])
        xT = sb("xT", [P, KD, NT])
        yT = sb("yT", [P, KD, NT + NS])
        lnp = sb("lnp", [P, 2, 2, D])
        wr = sb("wr", [P, WSLOT, KD, 512])
        bn = sb("bn", [P, 3, 2, 6])
        mv = sb("mv", [P, 3, 8])

        m0 = ExitStack()
        rows_v = sb("rows_v", [V_N, P], stack=m0)
        rows_dw = sb("rows_dw", [124, 2, P], stack=m0)
        rows_key = sb("rows_key", [P, 4, P], stack=m0)
        rows_sp = sb("rows_sp", [DB * PB, HALF], stack=m0)
        rows_sr = sb("rows_sr", [DB * RB, HALF], stack=m0)
        rows_sh = sb("rows_sh", [DB, HALF], stack=m0)
        pp = sb("pp", [P, JR, PB + SEQ], stack=m0)
        ps_ = sb("ps", [P, JR, DB, PB + DS], stack=m0)
        rp = sb("rp", [P, JR, RB + SEQ], stack=m0)
        rs = sb("rs", [P, JR, DB, RB + DS], stack=m0)
        dps = sb("dps", [P, JR, DB * PB], stack=m0)
        drs = sb("drs", [P, JR, DB * RB], stack=m0)
        h0 = sb("h0", [P, JR, DB], stack=m0)
        gg = sb("gg", [P, JR, NT], stack=m0)
        pooled = sb("pooled", [P, JR, NT], stack=m0)
        wa_ = sb("win_a", [P, PB + SEQ], stack=m0)
        wb_ = sb("win_b", [P, PB + SEQ], stack=m0)
        sa_ = sb("swin_a", [P, DB, PB + DS], stack=m0)
        sb_ = sb("swin_b", [P, DB, PB + DS], stack=m0)
        xc = sb("xc", [P, JR, NT], stack=m0)
        rg = sb("rg", [P, JR, NT], stack=m0)
        ig = sb("ig", [P, JR, NT], stack=m0)
        th = sb("th", [P, JR, NT], stack=m0)
        qv = sb("qv", [P, JR, NT], stack=m0)
        av = sb("av", [P, JR, NT], stack=m0)
        uv = sb("uv", [P, JR, NT], stack=m0)
        hT = sb("hT", [P, JR, NT], stack=m0)
        so = sb("so", [P, 6, HALF], stack=m0)
        m0.close()
        m1 = ExitStack()
        rows_sc = sb("rows_sc", [120, 2, D], stack=m1)
        cp = sb("cp", [P, KD, CB + SEQ], stack=m1)
        cs = sb("cs", [P, KD, DB, CB + DS], stack=m1)
        sg = sb("sg", [P, 2, NT], stack=m1)
        cT = sb("cT", [P, KD, NT], stack=m1)
        sq = sb("sq", [P, KD, NT], stack=m1)
        mub = sb("mub", [P, NT], stack=m1)
        rsb = sb("rsb", [P, 3, NT], stack=m1)
        so1 = sb("so1", [120, 2, 2, HALF], stack=m1)
        so1p = sb("so1p", [CB, 2, HALF], stack=m1)
        m1.close()
        mp = ExitStack()
        qT = sb("qT", [P, 16, SEQ], stack=mp)
        qS = sb("qS", [P, 8, 2, NS], stack=mp)
        sc = sb("sc", [P, 16, NK], stack=mp)
        sc2 = sb("sc2", [P, NK], stack=mp)
        tv = sb("tv", [P, 16, TOPK], stack=mp)
        ti = sb("ti", [P, 16, TOPK], U32, stack=mp)
        tif = sb("tif", [P, 16, TOPK], stack=mp)
        cand = sb("cand", [P, HEADS, TOPK, TOPK], stack=mp)
        cand2 = sb("cand2", [P, TOPK * TOPK], stack=mp)
        sv = sb("sv", [P, HEADS, TOPK], stack=mp)
        ci = sb("ci", [P, HEADS, TOPK], U32, stack=mp)
        cab = sb("cab", [P, 2, HEADS, TOPK], U32, stack=mp)
        cabf = sb("cabf", [P, 2, HEADS, TOPK], stack=mp)
        oh = cand
        e12 = sb("e12", [P, 2, HEADS, TOPK], stack=mp)
        eidx = sb("eidx", [P, 3, NK], I32, stack=mp)
        gate = sb("gate", [P, 3, HEADS, TOPK], stack=mp)
        gsm = sb("gsm", [P, 3, HEADS], stack=mp)
        actv = sb("actv", [P, 3, NK], stack=mp)
        acg = sb("acg", [P, 3, NK], stack=mp)
        stg = sb("stg", [P, 2, RING], I32, stack=mp)
        ring = sb("ring", [P, RING, D], stack=mp)
        acc = sb("acc", [P, 3, 2, D], stack=mp)
        mp.close()

        pb = [ctx.enter_context(nc.psum_tensor(f"bank{b}", [P, 512], F32)) for b in range(8)]

        s_mm = sem("s_mm")
        s_moved = [sem(f"s_moved{b}") for b in range(8)]
        s_x = sem("s_x")
        s_vec = sem("s_vec")
        s_key = sem("s_key")
        s_st = sem("s_st")
        s_bd = sem("s_bd")
        s_rows = sem("s_rows")
        s_dup = sem("s_dup")
        s_scv = sem("s_scv")
        s_w = [sem(f"s_w{i}") for i in range(WSLOT)]
        s_ln = [sem(f"s_ln{i}") for i in range(2)]
        s_out = sem("s_out")
        s_cst = sem("s_cst")
        s_bz = sem("s_bz")
        s_pw = sem("s_pw")
        s_pooled = sem("s_pooled")
        s_dv = sem("s_dv")
        s_inv = sem("s_inv")
        s_own = sem("s_own")
        s_lam1 = sem("s_lam1")
        s_lam2 = sem("s_lam2")
        s_spc = sem("s_spc")
        s_xc = sem("s_xc")
        s_th = sem("s_th")
        s_q2 = sem("s_q2")
        s_rt = sem("s_rt")
        s_h = sem("s_h")
        s_yb = sem("s_yb")
        s_var = sem("s_var")
        s_sd = sem("s_sd")
        s_xn = sem("s_xn")
        s_sub = sem("s_sub")
        s_ex = sem("s_ex")
        s_sel = sem("s_sel")
        s_e = sem("s_e")
        s_g = [sem(f"s_g{i}") for i in range(RING)]
        s_used = sem("s_used")
        s_turn = sem("s_turn")
        s_stg = sem("s_stg")
        s_act = sem("s_act")
        s_gel = sem("s_gel")
        s_accz = sem("s_accz")
        s_acc = sem("s_acc")
        s_sig = sem("s_sig")
        s_hist = sem("s_hist")
        s_cv = sem("s_cv")
        s_cm = sem("s_cm")
        s_csq = sem("s_csq")
        s_cve = sem("s_cve")
        s_csd = sem("s_csd")
        s_cn = sem("s_cn")
        s_silu = sem("s_silu")

        def moved(eng, name):
            g = GID[name]
            eng.wait_ge(s_moved[g % 8], g // 8 + 1)

        def filled(eng, name):
            eng.wait_ge(s_mm, GID[name] + 1)
            return pb[GID[name] % 8], s_moved[GID[name] % 8]

        def colblock(w, c):
            return w.rearrange("(k p) n -> p k n", p=P)[:, :, c * 512:(c + 1) * 512]

        WB = [(w_in_even[0], c) for c in range(3)] + [(w_out_even[0], c) for c in range(2)]
        WB += [(peer_wq[0], c) for c in range(4)]
        WB += [("glu", c) for c in range(4)] + [(w_pw[0], c) for c in range(2)]
        WB += [(peer_wq[1], c) for c in range(4)]
        W_IN, W_OUT, W_Q0, W_GLU, W_PW, W_Q1 = 0, 3, 5, 9, 13, 15

        LAST = [("z0", 4 * c + 3) for c in range(3)] + [("o", 0, 2, 1)] * 2 + [("q", 0, 4 * c + 3) for c in range(4)]
        LAST += [("z1", c, 3) for c in range(4)] + [("o", 1, 2, 1)] * 2 + [("q", 1, 4 * c + 3) for c in range(4)]

        ORDER = (("u", 0), ("u", 1), ("v", 0), ("u", 2), ("v", 1), ("v", 2))
        PHASES, at = [], 0
        for layer in range(2):
            for tab, n in ORDER:
                slots = TILES[n][1] * TOPK
                PHASES.append((layer, tab, n, slots, at))
                at += slots

        block = ctx.enter_context(nc.Block())

        @block.sync
        def _(sp):
            for n in range(2):
                sp.dma_start(x[:, n, :], x_prompt[0, n * P:(n + 1) * P, :]).then_inc(s_x, 16)
            for h in range(2):
                sp.dma_start(x[h * NS:(h + 1) * NS, 2, :], x_sample.rearrange("b s d -> (b s) d")).then_inc(s_x, 16)

            def weights(i):
                src, c = WB[i]
                if i >= WSLOT:
                    sp.wait_ge(s_mm, GID[LAST[i - WSLOT]] + 1)
                if src == "glu":
                    v = w_glu[0].rearrange("(k p) (a n) -> p k a n", p=P, a=2)[:, :, :, c * 256:(c + 1) * 256]
                    for a in range(2):
                        sp.dma_start(wr[:, i % WSLOT, :, a * 256:(a + 1) * 256], v[:, :, a, :]).then_inc(s_w[i % WSLOT], 16)
                else:
                    sp.dma_start(wr[:, i % WSLOT], colblock(src, c)).then_inc(s_w[i % WSLOT], 16)

            for i in range(WSLOT):
                weights(i)
            for src, r0, r1 in ((rnn_conv_w[0].rearrange("w (j p) -> (w j) p", p=P), V_CW, V_CB),
                                (rnn_conv_b.rearrange("a (j p) -> (a j) p", p=P), V_CB, V_BA),
                                (rg_ba.rearrange("a (j p) -> (a j) p", p=P), V_BA, V_BX),
                                (rg_bx.rearrange("a (j p) -> (a j) p", p=P), V_BX, V_LAM),
                                (rg_lambda.rearrange("a (j p) -> (a j) p", p=P), V_LAM, V_PS),
                                (pool_scale.rearrange("a (j p) -> (a j) p", p=P), V_PS, V_DB),
                                (dw_b.rearrange("a (j p) -> (a j) p", p=P), V_DB, V_CG),
                                (conv_ln_g.rearrange("a (j p) -> (a j) p", p=P), V_CG, V_CBT),
                                (conv_ln_b.rearrange("a (j p) -> (a j) p", p=P), V_CBT, V_N)):
                sp.dma_start(rows_v[r0:r1, :], src).then_inc(s_vec, 16)
            dwr = dw_w[0].rearrange("w (f p) -> (w f) p", p=P)
            for h in range(2):
                sp.dma_start(rows_dw[:, h, :], dwr[h * 124:(h + 1) * 124, :]).then_inc(s_vec, 16)
            for layer in range(2):
                sp.dma_start(rows_key[:, 2 * layer, :], peer_k1[layer]).then_inc(s_key, 16)
                sp.dma_start(rows_key[:, 2 * layer + 1, :], peer_k2[layer]).then_inc(s_key, 16)
            sp.dma_start(rows_sp[:], state_pool[0].rearrange("b t c -> (b t) c")).then_inc(s_st, 16)
            sp.dma_start(rows_sr[:], state_rnn_conv[0].rearrange("b t c -> (b t) c")).then_inc(s_st, 16)
            sp.dma_start(rows_sh[:], state_rnn_h[0]).then_inc(s_st, 16)
            sp.dma_start(poolw[:], pool_w[0].rearrange("g c d -> c g d")).then_inc(s_bd, 16)
            sp.wait_ge(s_bz, 2)
            for dst, src in ((bda, rg_wa), (bdx, rg_wx)):
                v = src[0].rearrange("(j h) i o -> h i j o", h=2)
                for h in range(2):
                    sp.dma_start(dst[64 * h:64 * h + 64, :, 64 * h:64 * h + 64], v[h]).then_inc(s_bd, 16)

            def ln_rows(i):
                if i >= 2:
                    sp.wait_ge(s_xn, 3 * (i - 1))
                layer = i // 2
                for j, v in enumerate((ln_ffn_g, ln_ffn_b) if i % 2 else (ln_mix_g, ln_mix_b)):
                    sp.dma_start(lnp[:, i % 2, j, :], v[layer:layer + 1, :].to_broadcast([P, D])).then_inc(s_ln[i % 2], 16)

            ln_rows(0)
            ln_rows(1)
            for i in range(WSLOT, W_OUT + 2):
                weights(i)
            for k, (dst, rows) in enumerate(((o_pool_p[0].rearrange("b t c -> (b t) c"), PB),
                                             (o_pool_s[0].rearrange("b t c -> (b t) c"), DB * PB),
                                             (o_rconv_p[0].rearrange("b t c -> (b t) c"), RB),
                                             (o_rconv_s[0].rearrange("b t c -> (b t) c"), DB * RB),
                                             (o_h_p[0], 1), (o_h_s[0], DB))):
                moved(sp, ("pst", k) if k < 4 else ("hst", k - 4))
                sp.dma_start(dst, so[0:rows, k, :]).then_inc(s_out, 16)
            for i in range(W_Q0, W_Q0 + 4):
                weights(i)
            ln_rows(2)
            for i in range(W_GLU, W_GLU + WSLOT):
                weights(i)
            ln_rows(3)
            sp.wait_ge(s_xn, 6)
            scr_ = state_conv[0].rearrange("b t c -> (b t) c")
            for p in range(2):
                sp.dma_start(rows_sc[:, p, :], scr_[120 * p:120 * p + 120, :]).then_inc(s_scv, 16)
            for i in range(W_GLU + WSLOT, W_PW + 2):
                weights(i)
            ocs = o_conv_s[0].rearrange("b t c -> (b t) c")
            for k in range(6):
                moved(sp, ("cst", k))
                if k < 2:
                    sp.dma_start(o_conv_p[0, 0, :, k * HALF:(k + 1) * HALF], so1p[:, k, :]).then_inc(s_out, 16)
                else:
                    p, q = (k - 2) // 2, k % 2
                    sp.dma_start(ocs[120 * p:120 * p + 120, q * HALF:(q + 1) * HALF], so1[:, p, q, :]).then_inc(s_out, 16)
            for i in range(W_Q1, W_Q1 + 4):
                weights(i)
            sp.wait_ge(s_xn, 12)
            for n in range(2):
                sp.dma_start(y_prompt[0, n * P:(n + 1) * P, :], x[:, n, :]).then_inc(s_out, 16)
            sp.dma_start(y_sample.rearrange("b s d -> (b s) d"), x[0:NS, 2, :]).then_inc(s_out, 16)
            sp.wait_ge(s_out, 16 * 15)

        @block.tensor
        def _(pe):
            todo = list(GROUPS)

            def begin(name):
                assert todo.pop(0) == name, name
                g = GID[name]
                if g >= 8:
                    pe.wait_ge(s_moved[g % 8], g // 8)
                return pb[g % 8]

            pe.wait_ge(s_cst, 5)
            pe.wait_ge(s_vec, 11 * 16)
            b = begin(("vec",))
            nc.tensor.transpose(b[:, 0:V_N], rows_v[:, :], ident[0:V_N, 0:V_N]).then_inc(s_mm, 1)
            for h in range(2):
                b = begin(("dw", h))
                nc.tensor.transpose(b[:, 0:124], rows_dw[:, h, :], ident[0:124, 0:124]).then_inc(s_mm, 1)
            pe.wait_ge(s_key, 64)
            b = begin(("key", 0))
            for i in range(4):
                last = nc.tensor.transpose(b[:, i * P:(i + 1) * P], rows_key[:, i, :], ident[:])
            last.then_inc(s_mm, 1)
            pe.wait_ge(s_st, 48)
            b = begin(("stp",))
            for j in range(JR):
                last = nc.tensor.transpose(b[:, j * 120:(j + 1) * 120], rows_sp[:, j * P:(j + 1) * P], ident[0:120, 0:120])
            last.then_inc(s_mm, 1)
            b = begin(("srh",))
            for j in range(JR):
                nc.tensor.transpose(b[:, j * 24:(j + 1) * 24], rows_sr[:, j * P:(j + 1) * P], ident[0:24, 0:24])
            for j in range(JR):
                last = nc.tensor.transpose(b[:, 96 + j * 8:104 + j * 8], rows_sh[:, j * P:(j + 1) * P], ident[0:8, 0:8])
            last.then_inc(s_mm, 1)

            def x_transposes(layer, part):
                if layer == 0 and part == 0:
                    pe.wait_ge(s_x, 64)
                for n in range(3):
                    if layer or part:
                        pe.wait_ge(s_xn, 3 * (2 * layer + part - 1) + n + 1)
                    rows = P if n < 2 else NS
                    for q in range(2):
                        b = begin(("xT", layer, part, n, q))
                        for i in range(4):
                            f = 4 * q + i
                            last = nc.tensor.transpose(b[:, i * rows:(i + 1) * rows],
                                                       x[0:rows, n, f * P:(f + 1) * P], ident[0:rows, 0:rows])
                        last.then_inc(s_mm, 1)

            def use_block(i):
                tot = sum(32 if WB[j][0] == "glu" else 16 for j in range(i % WSLOT, i + 1, WSLOT))
                pe.wait_ge(s_w[i % WSLOT], tot)
                return wr[:, i % WSLOT]

            def project(names, blk):
                w = use_block(blk)
                for i, name in enumerate(names):
                    b = begin(name)
                    for k in range(KD):
                        last = nc.tensor.matmul(b[:, 0:NT], w[:, k, i * P:(i + 1) * P], xT[:, k, :],
                                                start=(k == 0), stop=(k == KD - 1))
                    last.then_inc(s_mm, 1)

            def out_project(layer, blk):
                w = [use_block(blk), use_block(blk + 1)]
                for n in range(3):
                    if n == 2:
                        pe.wait_ge(s_dup, layer + 1)
                    for h in range(2):
                        b = begin(("o", layer, n, h))
                        for k in range(KD):
                            last = nc.tensor.matmul(b[:, :], yT[:, k, n * P:(n + 1) * P], w[h][:, k, :], start=(k == 0), stop=(k == KD - 1))
                        last.then_inc(s_mm, 1)

            def peer(layer):
                x_transposes(layer, 1)
                moved(pe, ("xT", layer, 1, 2, 1))
                for c in range(4):
                    project([("q", layer, 4 * c + i) for i in range(4)], (W_Q1 if layer else W_Q0) + c)
                moved(pe, ("q", layer, 15))
                for n, heads in TILES:
                    for i in range(heads // 2):
                        b = begin(("s", layer, n, i))
                        for j in range(4):
                            f = 4 * i + j
                            if n < 2:
                                lhs = qT[:, f, n * P:(n + 1) * P]
                            else:
                                lhs = qS[:, f].rearrange("p a t -> p (a t)")
                            last = nc.tensor.matmul(b[:, j * P:(j + 1) * P], lhs, keyT[:, 2 * layer + f % 2, :],
                                                    start=True, stop=True)
                        last.then_inc(s_mm, 1)
                pe.wait_ge(s_cst, 7)
                pe.wait_ge(s_acc, layer + 1)
                for h in range(2):
                    b = begin(("fold", layer, h))
                    nc.tensor.matmul(b[:, :], foldm[:], acc[:, 2, 0, h * 512:(h + 1) * 512],
                                     start=True, stop=True).then_inc(s_mm, 1)

            x_transposes(0, 0)
            moved(pe, ("xT", 0, 0, 2, 1))
            for c in range(3):
                project([("z0", 4 * c + i) for i in range(4)], W_IN + c)
            moved(pe, ("z0", 7))
            pe.wait_ge(s_rows, 2)
            for k, (buf, r0, rows) in enumerate(((pp, SEQ, PB), (dps, 0, DB * PB), (rp, SEQ, RB), (drs, 0, DB * RB))):
                b = begin(("pst", k))
                for j in range(JR):
                    last = nc.tensor.transpose(b[0:rows, j * P:(j + 1) * P], buf[:, j, r0:], ident[:])
                last.then_inc(s_mm, 1)
            pe.wait_ge(s_bd, 16 * 5)
            for j in range(JR):
                pe.wait_ge(s_pooled, j + 1)
                b = begin(("ya", j))
                nc.tensor.matmul(b[:, 0:NT], poolw[:, j, :], pooled[:, j, :], start=True, stop=True).then_inc(s_mm, 1)
            for j in range(JR):
                pe.wait_ge(s_xc, j + 1)
                for w, m in (("ga", bda), ("gx", bdx)):
                    b = begin((w, j))
                    nc.tensor.matmul(b[:, 0:NT], m[:, j, :], xc[:, j, :], start=True, stop=True).then_inc(s_mm, 1)
            pe.wait_ge(s_h, 1)
            for k in range(2):
                b = begin(("hst", k))
                for j in range(JR):
                    src = hT[:, j, SEQ - 1:SEQ] if k == 0 else hT[:, j, SEQ + DS - 1:NT:DS]
                    rows = 1 if k == 0 else DB
                    last = nc.tensor.transpose(b[0:rows, j * P:(j + 1) * P], src, ident[:])
                last.then_inc(s_mm, 1)
            moved(pe, ("ya", JR - 1))
            pe.wait_ge(s_yb, 1)
            out_project(0, W_OUT)
            peer(0)
            x_transposes(1, 0)
            pe.wait_ge(s_scv, 32)
            for p in range(2):
                for q in range(2):
                    b = begin(("scv", p, q))
                    for i in range(4):
                        f = 4 * q + i
                        last = nc.tensor.transpose(b[:, i * 120:(i + 1) * 120], rows_sc[:, p, f * P:(f + 1) * P],
                                                   ident[0:120, 0:120])
                    last.then_inc(s_mm, 1)
            moved(pe, ("xT", 1, 0, 2, 1))
            for c in range(4):
                project([("z1", c, i) for i in range(4)], W_GLU + c)
            moved(pe, ("z1", 3, 1))
            pe.wait_ge(s_rows, 3)
            for k in range(6):
                b = begin(("cst", k))
                for i in range(4):
                    if k < 2:
                        src, rows = cp[:, 4 * k + i, SEQ:], CB
                    else:
                        p, q = (k - 2) // 2, k % 2
                        src, rows = sq[:, 4 * q + i, p * 120:p * 120 + 120], 120
                    last = nc.tensor.transpose(b[0:rows, i * P:(i + 1) * P], src, ident[:])
                last.then_inc(s_mm, 1)
            pe.wait_ge(s_cv, 1)
            b = begin(("mu",))
            for f in range(KD):
                last = nc.tensor.matmul(b[:, 0:NT], mean_m[:], cT[:, f, :], start=(f == 0), stop=(f == KD - 1))
            last.then_inc(s_mm, 1)
            pe.wait_ge(s_csq, 1)
            b = begin(("var",))
            for f in range(KD):
                last = nc.tensor.matmul(b[:, 0:NT], mean_m[:], sq[:, f, :], start=(f == 0), stop=(f == KD - 1))
            last.then_inc(s_mm, 1)
            pe.wait_ge(s_silu, KD)
            out_project(1, W_PW)
            peer(1)
            assert not todo

        @block.scalar
        def _(act):
            A = nc.scalar.activation
            own = [0]

            def step(ins):
                own[0] += 1
                ins.then_inc(s_own, 1)
                act.wait_ge(s_own, own[0])

            b, free = filled(act, ("vec",))
            A(vecs[:], b[:, 0:V_N], ACT.Copy).then_inc(free, 1)
            for h in range(2):
                b, free = filled(act, ("dw", h))
                A(taps[:, h * 124:(h + 1) * 124], b[:, 0:124], ACT.Copy).then_inc(free, 1)
            b, free = filled(act, ("key", 0))
            A(keyT[:].rearrange("p a k -> p (a k)"), b[:], ACT.Copy).then_inc(free, 1)
            b, free = filled(act, ("stp",))
            A(ps_[:, :, :, 0:PB], b[:, 0:480].rearrange("p (j b t) -> p j b t", j=JR, b=DB), ACT.Copy).then_inc(free, 1)
            b, free = filled(act, ("srh",))
            A(rs[:, :, :, 0:RB], b[:, 0:96].rearrange("p (j b t) -> p j b t", j=JR, b=DB), ACT.Copy)
            A(h0[:], b[:, 96:128].rearrange("p (j b) -> p j b", j=JR), ACT.Copy).then_inc(free, 1)
            act.wait_ge(s_lam1, 1)
            A(sm[:, 4:8], sm[:, 0:4], ACT.Exp).then_inc(s_lam2, 1)

            def x_columns(layer, part):
                for n in range(3):
                    cols = P if n < 2 else NS
                    for q in range(2):
                        b, free = filled(act, ("xT", layer, part, n, q))
                        A(xT[:, 4 * q:4 * q + 4, n * P:n * P + cols],
                          b[:, 0:4 * cols].rearrange("p (f t) -> p f t", f=4), ACT.Copy).then_inc(free, 1)

            def roots(i):
                for n in range(3):
                    act.wait_ge(s_var, 3 * i + n + 1)
                    A(mv[:, n, 3:4], mv[:, n, 2:3], ACT.Sqrt).then_inc(s_sd, 1)

            def peer(layer):
                x_columns(layer, 1)
                act.wait_ge(s_out, 16 * 6 * (layer + 1))
                for ft in range(16):
                    b, free = filled(act, ("q", layer, ft))
                    A(qT[:, ft, :], b[:, 0:SEQ], ACT.Copy)
                    A(qS[:, ft % 8, ft // 8, :], b[:, SEQ:NT], ACT.Copy).then_inc(free, 1)
                for n, heads in TILES:
                    if n:
                        act.wait_ge(s_sel, 3 * layer + n)
                    for i in range(heads // 2):
                        b, free = filled(act, ("s", layer, n, i))
                        A(sc[:, 4 * i:4 * i + 4, :].rearrange("p a k -> p (a k)"), b[:], ACT.Copy).then_inc(free, 1)
                    act.wait_ge(s_sub, 3 * layer + n + 1)
                    A(gate[:, n, 0:heads, :], gate[:, n, 0:heads, :], ACT.Exp).then_inc(s_ex, 1)
                done = 0
                for l, tab, n, slots, _ in PHASES:
                    if l == layer and tab == "u":
                        done += 1
                        act.wait_ge(s_act, 3 * layer + done)
                        A(acg[:, n, 0:slots], actv[:, n, 0:slots], ACT.Gelu_apprx_tanh).then_inc(s_gel, 1)
                roots(2 * layer + 1)

            x_columns(0, 0)
            for ft in range(12):
                b, free = filled(act, ("z0", ft))
                if ft < 8:
                    dp, ds_, hist = (pp, ps_, PB) if ft < 4 else (rp, rs, RB)
                    A(dp[:, ft % 4, hist:], b[:, 0:SEQ], ACT.Copy)
                    A(ds_[:, ft % 4, :, hist:], b[:, SEQ:NT].rearrange("p (b s) -> p b s", b=DB), ACT.Copy).then_inc(free, 1)
                else:
                    A(gg[:, ft - 8, :], b[:, 0:NT], ACT.Gelu_apprx_tanh).then_inc(free, 1)
            for k, rows in enumerate((PB, DB * PB, RB, DB * RB)):
                b, free = filled(act, ("pst", k))
                A(so[0:rows, k, :], b[0:rows, :], ACT.Copy).then_inc(free, 1)
            for j in range(JR):
                b, free = filled(act, ("ya", j))
                A(yT[:, j, 0:NT], b[:, 0:NT], ACT.Identity, scale=vecs[:, V_PS + j:V_PS + j + 1]).then_inc(free, 1)
            for j in range(JR):
                for w, dst, v in (("ga", rg, V_BA), ("gx", ig, V_BX)):
                    b, free = filled(act, (w, j))
                    A(dst[:, j, :], b[:, 0:NT], ACT.Sigmoid, bias=vecs[:, v + j:v + j + 1]).then_inc(free, 1)
            act.wait_ge(s_spc, 1)
            moved(act, ("gx", JR - 1))
            for j in range(JR):
                A(th[:, j, :], rg[:, j, :], ACT.Tanh, scale=spc[:, j:j + 1]).then_inc(s_th, 1)
            act.wait_ge(s_q2, 1)
            A(th[:], rg[:], ACT.Sqrt).then_inc(s_rt, 1)
            for k, rows in enumerate((1, DB)):
                b, free = filled(act, ("hst", k))
                A(so[0:rows, 4 + k, :], b[0:rows, :], ACT.Copy).then_inc(free, 1)
            roots(0)
            peer(0)
            x_columns(1, 0)
            for p in range(2):
                for q in range(2):
                    b, free = filled(act, ("scv", p, q))
                    for i in range(4):
                        last = A(cs[:, 4 * q + i, 4 * p:4 * p + 4, 0:CB],
                                 b[:, 120 * i:120 * i + 120].rearrange("p (b t) -> p b t", b=4), ACT.Copy)
                    last.then_inc(free, 1)
            for c in range(4):
                if c:
                    moved(act, ("z1", c - 1, 1))
                for i in range(2):
                    b, free = filled(act, ("z1", c, 2 + i))
                    A(sg[:, i, :], b[:, 0:NT], ACT.Sigmoid).then_inc(free, 1)
            for k in range(6):
                b, free = filled(act, ("cst", k))
                rows = CB if k < 2 else 120
                dst = so1p[:, k, :] if k < 2 else so1[:, (k - 2) // 2, k % 2, :]
                A(dst, b[0:rows, :], ACT.Copy).then_inc(free, 1)
            b, free = filled(act, ("mu",))
            A(mub[:], b[:, 0:NT], ACT.Copy).then_inc(free, 1)
            act.wait_ge(s_cm, 1)
            A(sq[:], cT[:], ACT.Square).then_inc(s_csq, 1)
            act.wait_ge(s_cve, 1)
            A(rsb[:, 1, :], rsb[:, 0, :], ACT.Sqrt).then_inc(s_csd, 1)
            act.wait_ge(s_cn, 1)
            for f in range(KD):
                A(yT[:, f, 0:NT], cT[:, f, :], ACT.Silu, bias=vecs[:, V_CBT + f:V_CBT + f + 1],
                  scale=vecs[:, V_CG + f:V_CG + f + 1]).then_inc(s_silu, 1)
            roots(2)
            peer(1)

        @block.vector
        def _(dve):
            V = nc.vector
            count = {}

            def step(ins, s=s_dv):
                count[s.name] = count.get(s.name, 0) + 1
                ins.then_inc(s, 1)
                dve.wait_ge(s, count[s.name])

            dve.sem_inc(s_used, RING)
            dve.wait_ge(s_cst, 6)
            step(V.tensor_copy(iota_f[:], iota_i[:]))
            for j in range(JR):
                step(V.tensor_scalar(inv_cnt[:, j, :], iota_f[:], 1.0, float(2 << j), ALU.add, ALU.min))
            step(V.reciprocal(inv_cnt[:], inv_cnt[:]), s_inv)
            moved(dve, ("vec",))
            lam = vecs[:, V_LAM:V_LAM + JR]
            step(V.tensor_scalar(sm[:, 8:12], lam, -1.0, None, ALU.mult))
            step(V.tensor_tensor(sm[:, 0:4], sm[:, 8:12], lam, ALU.min), s_lam1)
            dve.wait_ge(s_lam2, 1)
            e, z, s2, p = sm[:, 4:8], sm[:, 12:16], sm[:, 16:20], sm[:, 20:24]
            step(V.tensor_scalar(z, e, 2.0, None, ALU.add))
            step(V.reciprocal(z, z))
            step(V.tensor_tensor(z, z, e, ALU.mult))
            step(V.tensor_tensor(s2, z, z, ALU.mult))
            step(V.tensor_scalar(p, s2, 1.0 / 17, None, ALU.mult))
            for c in (15, 13, 11, 9, 7, 5, 3):
                step(V.scalar_tensor_tensor(p, p, 1.0 / c, s2, ALU.add, ALU.mult))
            step(V.scalar_tensor_tensor(p, p, 1.0, z, ALU.add, ALU.mult))
            step(V.tensor_scalar(sm[:, 8:12], sm[:, 8:12], 0.0, 4.0, ALU.max, ALU.mult))
            step(V.scalar_tensor_tensor(spc[:], p, 8.0, sm[:, 8:12], ALU.mult, ALU.add), s_spc)

            dve.wait_ge(s_bz, 4)
            moved(dve, ("srh",))
            for j in range(JR):
                moved(dve, ("z0", 4 + j))
                bias = vecs[:, V_CB + j:V_CB + j + 1]
                tap = [vecs[:, V_CW + 4 * w + j:V_CW + 4 * w + j + 1] for w in range(4)]
                dp, dc = xc[:, j, 0:SEQ], xc[:, j, SEQ:NT].rearrange("p (b s) -> p b s", b=DB)
                step(V.tensor_scalar(dp, rp[:, j, 0:SEQ], tap[0], bias, ALU.mult, ALU.add))
                step(V.tensor_scalar(dc, rs[:, j, :, 0:DS], tap[0], bias, ALU.mult, ALU.add))
                for w in range(1, 4):
                    step(V.scalar_tensor_tensor(dp, rp[:, j, w:w + SEQ], tap[w], dp, ALU.mult, ALU.add))
                    step(V.scalar_tensor_tensor(dc, rs[:, j, :, w:w + DS], tap[w], dc, ALU.mult, ALU.add),
                         s_xc if w == 3 else s_dv)
            dve.wait_ge(s_th, JR)
            step(V.tensor_scalar(uv[:], th[:], 1.0, None, ALU.add))
            step(V.reciprocal(uv[:], uv[:]))
            step(V.scalar_tensor_tensor(qv[:], th[:], 2.0, uv[:], ALU.mult, ALU.mult))
            step(V.tensor_scalar(av[:], qv[:], -1.0, 1.0, ALU.mult, ALU.add))
            step(V.tensor_scalar(uv[:], qv[:], -1.0, 2.0, ALU.mult, ALU.add))
            step(V.tensor_tensor(rg[:], qv[:], uv[:], ALU.mult), s_q2)
            step(V.tensor_tensor(ig[:], ig[:], xc[:], ALU.mult))
            dve.wait_ge(s_rt, 1)
            step(V.tensor_tensor(uv[:], th[:], ig[:], ALU.mult))
            ap, up = [t[:, :, SEQ:NT].rearrange("p j (b s) -> p j b s", b=DB)[:, :, :, 0] for t in (av, uv)]
            step(V.tensor_tensor(h0[:], h0[:], ap, ALU.mult))
            step(V.tensor_tensor(up, up, h0[:], ALU.add))
            step(V.memset(ap, 0.0))
            for j in range(JR):
                step(V.tensor_tensor_scan(hT[:, j, 0:SEQ], av[:, j, 0:SEQ], uv[:, j, 0:SEQ], 0.0, ALU.mult, ALU.add))
                last = V.tensor_tensor_scan(hT[:, j, SEQ:NT], av[:, j, SEQ:NT], uv[:, j, SEQ:NT], 0.0, ALU.mult, ALU.add)
                step(last, s_h if j == JR - 1 else s_dv)
            moved(dve, ("z0", 11))
            step(V.tensor_tensor(yT[:, JR:KD, 0:NT], hT[:], gg[:], ALU.mult), s_yb)

            def layer_norm(i):
                layer = i // 2
                dve.wait_ge(s_ln[i % 2], 32 * (i // 2 + 1))
                for n in range(3):
                    for h in range(2):
                        xs = x[:, n, h * 512:(h + 1) * 512]
                        if i % 2 == 0 or n == 2:
                            b, free = filled(dve, ("o", layer, n, h) if i % 2 == 0 else ("fold", layer, h))
                            V.scalar_tensor_tensor(xs, xs, ALPHA, b[:], ALU.mult, ALU.add).then_inc(free, 1)
                            moved(dve, ("o", layer, n, h) if i % 2 == 0 else ("fold", layer, h))
                        else:
                            for a in range(2):
                                step(V.scalar_tensor_tensor(xs, xs, 1.0 if a else ALPHA, acc[:, n, a, h * 512:(h + 1) * 512],
                                                            ALU.mult, ALU.add))
                        step(V.bn_stats(bn[:, n, h, :], xs))
                    step(V.bn_aggr(mv[:, n, 0:2], bn[:, n, :, :].rearrange("p h c -> p (h c)")))
                    step(V.tensor_scalar(mv[:, n, 2:3], mv[:, n, 1:2], EPS, None, ALU.add), s_var)
                    dve.wait_ge(s_sd, 3 * i + n + 1)
                    inverse(mv[:, n, 3:4], mv[:, n, 2:3], mv[:, n, 4:5], mv[:, n, 5:6])
                    step(V.tensor_scalar(x[:, n, :], x[:, n, :], mv[:, n, 0:1], mv[:, n, 4:5], ALU.subtract, ALU.mult))
                    step(V.tensor_tensor(x[:, n, :], x[:, n, :], lnp[:, i % 2, 0, :], ALU.mult))
                    step(V.tensor_tensor(x[:, n, :], x[:, n, :], lnp[:, i % 2, 1, :], ALU.add), s_xn)

            def inverse(root, var, r, t):
                step(V.reciprocal(r, root))
                step(V.tensor_tensor(t, r, r, ALU.mult))
                step(V.tensor_tensor(t, t, var, ALU.mult))
                step(V.tensor_scalar(t, t, -0.5, 1.5, ALU.mult, ALU.add))
                step(V.tensor_tensor(r, r, t, ALU.mult))

            def top16(vals, idx, src, spare):
                step(V.max(vals[:, 0:8], src))
                step(V.max_index(idx[:, 0:8], vals[:, 0:8], src))
                step(V.match_replace(spare, vals[:, 0:8], src, -3.0e38))
                step(V.max(vals[:, 8:16], spare))
                step(V.max_index(idx[:, 8:16], vals[:, 8:16], spare))

            def choose(layer, n, heads):
                for f in range(2 * heads):
                    moved(dve, ("s", layer, n, f // 4))
                    top16(tv[:, f, :], ti[:, f, :], sc[:, f, :], sc2[:])
                dve.sem_inc(s_sel, 1)
                g = 2 * heads
                step(V.tensor_copy(tif[:, 0:g, :], ti[:, 0:g, :]))
                v1 = tv[:, 0:g:2, :].unsqueeze(3).to_broadcast([P, heads, TOPK, TOPK])
                v2 = tv[:, 1:g:2, :].unsqueeze(2).to_broadcast([P, heads, TOPK, TOPK])
                step(V.tensor_tensor(cand[:, 0:heads], v1, v2, ALU.add))
                for h in range(heads):
                    top16(sv[:, h, :], ci[:, h, :], cand[:, h].rearrange("p a b -> p (a b)"), cand2[:])
                step(V.tensor_tensor(gate[:, n, 0:heads, :], sv[:, 0:heads, :],
                                     sv[:, 0:heads, 0:1].to_broadcast([P, heads, TOPK]), ALU.subtract), s_sub)
                step(V.tensor_single_scalar(cab[:, 0, 0:heads, :], ci[:, 0:heads, :], 4, ALU.logical_shift_right))
                step(V.tensor_single_scalar(cab[:, 1, 0:heads, :], ci[:, 0:heads, :], 15, ALU.bitwise_and))
                step(V.tensor_copy(cabf[:, :, 0:heads, :], cab[:, :, 0:heads, :]))
                for a in range(2):
                    o = oh[:, 0:heads]
                    step(V.tensor_tensor(o, cabf[:, a, 0:heads, :].unsqueeze(3).to_broadcast([P, heads, TOPK, TOPK]),
                                         iota_f[:].unsqueeze(1).unsqueeze(1).to_broadcast([P, heads, TOPK, TOPK]),
                                         ALU.is_equal))
                    step(V.tensor_tensor(o, o, tif[:, a:g:2, :].unsqueeze(2).to_broadcast([P, heads, TOPK, TOPK]), ALU.mult))
                    step(V.tensor_reduce(e12[:, a, 0:heads, :], o, AX.X, ALU.add))
                step(V.tensor_scalar(e12[:, 0, 0:heads, :], e12[:, 0, 0:heads, :], float(NK), float(layer * NE),
                                     ALU.mult, ALU.add))
                step(V.tensor_tensor(eidx[:, n, 0:heads * TOPK].rearrange("p (h k) -> p h k", h=heads),
                                     e12[:, 0, 0:heads, :], e12[:, 1, 0:heads, :], ALU.add), s_e)
                dve.wait_ge(s_ex, 3 * layer + n + 1)
                step(V.tensor_reduce(gsm[:, n, 0:heads], gate[:, n, 0:heads, :], AX.X, ALU.add))
                step(V.reciprocal(gsm[:, n, 0:heads], gsm[:, n, 0:heads]))
                step(V.tensor_tensor(gate[:, n, 0:heads, :], gate[:, n, 0:heads, :],
                                     gsm[:, n, 0:heads].unsqueeze(2).to_broadcast([P, heads, TOPK]), ALU.mult))

            def use_rows(tab, n, slots, start):
                with dve.Fori(0, slots // RING) as i:
                    for k in range(RING):
                        dve.wait_ge(s_g[k], i * 16 + (start // RING + 1) * 16)
                        dve.wait_ge(s_used, i * RING + (RING + start + k - 1))
                        col = bass.ds(i * RING + k, 1)
                        if tab == "u":
                            V.scalar_tensor_tensor(acc[:, n, k % 2, :], ring[:, k, :], 1.0, x[:, n, :], ALU.mult, ALU.mult,
                                                   accum_out=actv[:, n, col]).then_inc(s_used, 1)
                        else:
                            V.scalar_tensor_tensor(acc[:, n, k % 2, :], ring[:, k, :], actv[:, n, col], acc[:, n, k % 2, :],
                                                   ALU.mult, ALU.add).then_inc(s_used, 1)
                dve.wait_ge(s_used, RING + start + slots)

            def peer(layer):
                for n, heads in TILES:
                    choose(layer, n, heads)
                done = 0
                for l, tab, n, slots, start in PHASES:
                    if l != layer:
                        continue
                    use_rows(tab, n, slots, start)
                    if tab == "u":
                        done += 1
                        step(V.memset(acc[:, n], 0.0), s_act)
                        dve.wait_ge(s_gel, 3 * layer + done)
                        step(V.tensor_tensor(actv[:, n, 0:slots], acg[:, n, 0:slots],
                                             gate[:, n].rearrange("p h k -> p (h k)")[:, 0:slots], ALU.mult))
                step(V.tensor_tensor(acc[:, 2, 0, :], acc[:, 2, 0, :], acc[:, 2, 1, :], ALU.add), s_acc)
                layer_norm(2 * layer + 1)

            layer_norm(0)
            peer(0)
            moved(dve, ("scv", 1, 1))
            dve.wait_ge(s_hist, 1)
            for c in range(4):
                moved(dve, ("z1", c, 3))
                for i in range(2):
                    f = 2 * c + i
                    b, free = filled(dve, ("z1", c, i))
                    V.tensor_tensor(cp[:, f, CB:], b[:, 0:SEQ], sg[:, i, 0:SEQ], ALU.mult)
                    V.tensor_tensor(cs[:, f, :, CB:], b[:, SEQ:NT].rearrange("p (b s) -> p b s", b=DB),
                                    sg[:, i, SEQ:NT].rearrange("p (b s) -> p b s", b=DB), ALU.mult).then_inc(free, 1)
            moved(dve, ("z1", 3, 1))
            for f in range(KD):
                tap = [taps[:, w * KD + f:w * KD + f + 1] for w in range(CW)]
                dp, dc = cT[:, f, 0:SEQ], cT[:, f, SEQ:NT].rearrange("p (b s) -> p b s", b=DB)
                bias = vecs[:, V_DB + f:V_DB + f + 1]
                step(V.tensor_scalar(dp, cp[:, f, 0:SEQ], tap[0], bias, ALU.mult, ALU.add))
                step(V.tensor_scalar(dc, cs[:, f, :, 0:DS], tap[0], bias, ALU.mult, ALU.add))
                for w in range(1, CW):
                    step(V.scalar_tensor_tensor(dp, cp[:, f, w:w + SEQ], tap[w], dp, ALU.mult, ALU.add))
                    step(V.scalar_tensor_tensor(dc, cs[:, f, :, w:w + DS], tap[w], dc, ALU.mult, ALU.add),
                         s_cv if f == KD - 1 and w == CW - 1 else s_dv)
            moved(dve, ("mu",))
            step(V.tensor_tensor(cT[:], cT[:], mub[:].unsqueeze(1).to_broadcast([P, KD, NT]), ALU.subtract), s_cm)
            b, free = filled(dve, ("var",))
            V.tensor_scalar(rsb[:, 0, :], b[:, 0:NT], EPS, None, ALU.add).then_inc(free, 1)
            moved(dve, ("var",))
            dve.sem_inc(s_cve, 1)
            dve.wait_ge(s_csd, 1)
            inverse(rsb[:, 1, :], rsb[:, 0, :], rsb[:, 2, :], mub[:])
            step(V.tensor_tensor(cT[:], cT[:], rsb[:, 2, :].unsqueeze(1).to_broadcast([P, KD, NT]), ALU.mult), s_cn)
            layer_norm(2)
            peer(1)

        @block.gpsimd
        def _(pool):
            G = nc.gpsimd
            G.memset(ident[:], 0.0).then_inc(s_cst, 1)
            G.memset(foldm[:], 0.0).then_inc(s_cst, 1)
            G.memset(mean_m[:], 1.0 / D).then_inc(s_cst, 1)
            pool.wait_ge(s_cst, 2)
            G.affine_select(out=ident[:], in_=ident[:], compare_op=ALU.not_equal, fill=1.0, base=0,
                            pattern=[[-1, P]], channel_multiplier=1).then_inc(s_cst, 1)
            f = foldm[:].rearrange("p (h q) -> p h q", h=2)
            G.affine_select(out=f, in_=f, compare_op=ALU.not_equal, fill=1.0, base=0,
                            pattern=[[0, 2], [-1, NS]], channel_multiplier=1).then_inc(s_cst, 1)
            pool.wait_ge(s_cst, 5)
            G.iota(iota_i[:], pattern=[[1, 16]], base=0, channel_multiplier=0).then_inc(s_cst, 1)
            G.affine_select(out=f, in_=f, compare_op=ALU.not_equal, fill=1.0, base=-NS,
                            pattern=[[0, 2], [-1, NS]], channel_multiplier=1).then_inc(s_cst, 1)
            G.memset(bda[:], 0.0).then_inc(s_bz, 1)
            G.memset(bdx[:], 0.0).then_inc(s_bz, 1)
            G.memset(pp[:, :, 0:PB], 0.0).then_inc(s_bz, 1)
            G.memset(rp[:, :, 0:RB], 0.0).then_inc(s_bz, 1)
            pool.wait_ge(s_bz, 4)
            n_pw = [0]

            def step(ins):
                n_pw[0] += 1
                ins.then_inc(s_pw, 1)
                pool.wait_ge(s_pw, n_pw[0])

            moved(pool, ("z0", 7))
            moved(pool, ("srh",))
            for dst, src, rows in ((dps, ps_, PB), (drs, rs, RB)):
                for j in range(JR):
                    step(G.tensor_copy(dst[:, j, :].rearrange("p (b t) -> p b t", b=DB), src[:, j, :, DS:]))
                pool.sem_inc(s_rows, 1)
            pool.wait_ge(s_inv, 1)
            moved(pool, ("stp",))
            for j in range(JR):
                moved(pool, ("z0", j))
                w = 2 << j
                src_p, src_s = pp[:, j, :], ps_[:, j]
                for lev in range(j + 1):
                    d, lo = 1 << lev, (2 << lev) - 1
                    dst_p, dst_s = (wa_, sa_) if lev % 2 == 0 else (wb_, sb_)
                    step(G.tensor_tensor(dst_p[:, lo:], src_p[:, lo:], src_p[:, lo - d:PB + SEQ - d], ALU.add))
                    step(G.tensor_tensor(dst_s[:, :, lo:], src_s[:, :, lo:], src_s[:, :, lo - d:PB + DS - d], ALU.add))
                    src_p, src_s = dst_p[:, :], dst_s[:, :, :]
                step(G.tensor_tensor(pooled[:, j, 0:16], src_p[:, PB:PB + 16], inv_cnt[:, j, :], ALU.mult))
                step(G.tensor_scalar(pooled[:, j, 16:SEQ], src_p[:, PB + 16:], 1.0 / w, None, ALU.mult))
                dst = pooled[:, j, SEQ:NT].rearrange("p (b s) -> p b s", b=DB)
                step(G.tensor_scalar(dst, src_s[:, :, PB:], 1.0 / w, None, ALU.mult))
                step(G.tensor_tensor(pooled[:, j, 0:SEQ], pooled[:, j, 0:SEQ], pp[:, j, PB:], ALU.subtract))
                G.tensor_tensor(dst, dst, ps_[:, j, :, PB:], ALU.subtract).then_inc(s_pooled, 1)

            moved(pool, ("ya", JR - 1))
            pool.wait_ge(s_yb, 1)
            G.tensor_copy(yT[:, :, NT:], yT[:, :, SEQ:NT]).then_inc(s_dup, 1)

            def odd_mixer():
                pool.wait_ge(s_xn, 6)
                G.memset(cp[:, :, 0:CB], 0.0).then_inc(s_hist, 1)
                moved(pool, ("z1", 3, 1))
                for f in range(KD):
                    last = G.tensor_copy(sq[:, f, 0:DB * CB].rearrange("p (b t) -> p b t", b=DB), cs[:, f, :, DS:])
                last.then_inc(s_rows, 1)
                pool.wait_ge(s_silu, KD)
                G.tensor_copy(yT[:, :, NT:], yT[:, :, SEQ:NT]).then_inc(s_dup, 1)

            tables = {"u": peer_u.rearrange("l e d -> (l e) d"), "v": peer_v.rearrange("l e d -> (l e) d")}
            for layer, tab, n, slots, start in PHASES:
                if layer == 1 and tab == "u" and n == 0:
                    odd_mixer()
                pool.wait_ge(s_e, 3 * layer + n + 1)
                with pool.Fori(0, slots // (2 * RING)) as i:
                    for h in range(2):
                        G.tensor_copy(stg[:, h, :], eidx[:, n, bass.ds(i * 2 * RING + h * RING, RING)]).then_inc(s_stg, 1)
                        pool.wait_ge(s_stg, i * 2 + (start // RING + h + 1))
                        for k in range(RING):
                            pool.wait_ge(s_used, i * 2 * RING + (start + h * RING + k + 1))
                            pool.sem_inc(s_turn, 1)
                            G.indirect_dma_start(ring[:, k, :], None, tables[tab],
                                                 bass.IndirectOffsetOnAxis(stg[:, h, k:k + 1], 0)).then_inc(s_g[k], 16)


_INS = ['x_prompt', 'x_sample', 'state_pool', 'state_rnn_conv', 'state_rnn_h', 'state_conv',
        'w_in_even', 'pool_w', 'pool_scale', 'rnn_conv_w', 'rnn_conv_b', 'rg_wa', 'rg_ba', 'rg_wx', 'rg_bx',
        'rg_lambda', 'w_out_even', 'w_glu', 'dw_w', 'dw_b', 'conv_ln_g', 'conv_ln_b', 'w_pw',
        'peer_wq', 'peer_k1', 'peer_k2', 'peer_u', 'peer_v', 'ln_mix_g', 'ln_mix_b', 'ln_ffn_g', 'ln_ffn_b']
_OUTS = [(1, SEQ, D), (DB, DS, D), (1, 1, PB, HALF), (1, 1, RB, HALF), (1, 1, HALF), (1, 1, CB, D),
         (1, DB, PB, HALF), (1, DB, RB, HALF), (1, DB, HALF), (1, DB, CB, D)]


def kernel(**inputs):
    import numpy as _np
    import concourse.bacc as _bacc
    from concourse import mybir as _mybir
    from concourse.bass_utils import run_bass_kernel_spmd as _run

    nc = _bacc.Bacc("TRN2", target_bir_lowering=False, num_devices=1)
    arrays, args = {}, []
    for name in _INS:
        a = _np.ascontiguousarray(inputs[name])
        arrays[f"in_{name}_dram"] = a
        args.append(nc.dram_tensor(f"in_{name}_dram", a.shape, _mybir.dt.from_np(a.dtype), kind="ExternalInput").ap())
    for i, shape in enumerate(_OUTS):
        args.append(nc.dram_tensor(f"out_{i}_dram", shape, _mybir.dt.float32, kind="ExternalOutput").ap())
    build(nc, *args)
    r = _run(nc, [arrays], core_ids=[0])
    return tuple(r.results[0][f"out_{i}_dram"] for i in range(len(_OUTS)))
```

```python
import concourse.bass as bass
from concourse import mybir
from contextlib import ExitStack
import numpy as np

F32 = mybir.dt.float32
I32 = mybir.dt.int32
U32 = mybir.dt.uint32
ALU = mybir.AluOpType
ACT = mybir.ActivationFunctionType
AX = mybir.AxisListType

P = 128
D = 1024
KD = D // P
SEQ, DB, DS = 256, 8, 8
NS = DB * DS
NT = SEQ + NS
HALF = D // 2
JR = HALF // P
PB, RB, CB = 15, 3, 30
CW = 31
HEADS, NK, TOPK = 8, 128, 16
NE = NK * NK
ALPHA = (2.0 * 2) ** 0.25
EPS = 1e-5
RING = 8
WSLOT, WC = 3, 256
SLOTS = 3
PE_F = 5
DIAG = 4
V_CW, V_CB, V_BA, V_BX, V_LAM, V_PS, V_DB, V_CG, V_CBT, V_N = 0, 16, 20, 24, 28, 32, 36, 44, 52, 60

S, Q = 0, 1
COLS = (NS, SEQ)
TILES = ((2,), (0, 1))
HEADS_OF = (8, 8, 4)
STREAM = (Q, Q, S)


def width(n):
    return NS if n == 2 else P


NORMS = [(0, 2), (0, 0), (0, 1), (1, 2), (2, 2), (1, 0), (1, 1), (2, 0), (2, 1), (3, 2), (3, 0), (3, 1)]
CHOICES = [(0, 2), (0, 0), (0, 1), (1, 2), (1, 0), (1, 1)]


def gather_phases():
    out, at = [], 0
    for layer in range(2):
        for tab, n in (("u", 2), ("v", 2), ("u", 0), ("u", 1), ("v", 0), ("v", 1)):
            slots = HEADS_OF[n] * TOPK
            out.append((layer, tab, n, slots, at))
            at += slots
    return out


PHASES = gather_phases()


def psum_groups():
    g = [("vec",), ("dw", 0), ("dw", 1), ("key",), ("stp",), ("srh",)]

    def x_turned(layer, part, tiles):
        return [("xT", layer, part, n, q) for n in tiles for q in range(2)]

    def projected_out(layer, st):
        return [("o", layer, n, blk) for blk in range(D // WC) for n in TILES[st]]

    def even_mixer(st):
        return (x_turned(0, 0, TILES[st]) + [("z0", st, ft) for ft in range(12)] + [("st0", st, k) for k in range(2)]
                + [("ya", st, j) for j in range(JR)] + [(w, st, j) for j in range(JR) for w in ("ga", "gx")]
                + [("h0", st)] + projected_out(0, st))

    def odd_mixer(st):
        out = x_turned(1, 0, TILES[st])
        if st == S:
            out += [("scv", p, q) for p in range(2) for q in range(2)]
        out += [("z1", st, f) for f in range(KD)] + [("cst", st, k) for k in range(4 if st == S else 2)]
        out += [("cv", st, f) for f in range(KD if st == S else PE_F)] + [("mu", st), ("var", st)]
        return out + projected_out(1, st)

    def front(layer, n):
        return (x_turned(layer, 1, (n,)) + [("q", layer, n, c) for c in range(4)]
                + [("s", layer, n, i) for i in range(HEADS_OF[n] // 2)])

    for layer, mixer in ((0, even_mixer), (1, odd_mixer)):
        g += mixer(S) + front(layer, 2) + mixer(Q) + front(layer, 0) + front(layer, 1)
        g += [("fold", layer, h) for h in range(2)]
    return g


GROUPS = psum_groups()
GID = {name: i for i, name in enumerate(GROUPS)}


def weight_blocks():
    out = []
    for layer in range(2):
        q = [[("q", layer, c, ("q", layer, n, c // 2)) for c in range(8)] for n in range(3)]
        for st in (S, Q):
            if layer == 0:
                out += [("in", 0, c, ("z0", st, 2 * c + 1)) for c in range(6)]
            else:
                out += [("glu", 0, c, ("z1", st, c)) for c in range(KD)]
            out += [("out" if layer == 0 else "pw", 0, c, ("o", layer, TILES[st][-1], c)) for c in range(4)]
            for n in TILES[st]:
                out += q[n]
    return out


BLOCKS = weight_blocks()


def build(nc, x_prompt, x_sample, state_pool, state_rnn_conv, state_rnn_h, state_conv,
          w_in_even, pool_w, pool_scale, rnn_conv_w, rnn_conv_b, rg_wa, rg_ba, rg_wx, rg_bx,
          rg_lambda, w_out_even, w_glu, dw_w, dw_b, conv_ln_g, conv_ln_b, w_pw,
          peer_wq, peer_k1, peer_k2, peer_u, peer_v, ln_mix_g, ln_mix_b, ln_ffn_g, ln_ffn_b,
          y_prompt, y_sample, o_pool_p, o_rconv_p, o_h_p, o_conv_p, o_pool_s, o_rconv_s, o_h_s, o_conv_s):
    ctx = ExitStack()
    with ctx:
        def sb(name, shape, dt=F32, stack=ctx):
            return stack.enter_context(nc.sbuf_tensor(name, shape, dt))

        def sem(name):
            return ctx.enter_context(nc.semaphore(name))

        ident = sb("ident", [P, P])
        foldm = sb("foldm", [P, P])
        mean_m = sb("mean_m", [P, P])
        iota_i = sb("iota_i", [P, 16], I32)
        iota_f = sb("iota_f", [P, 16])
        inv_cnt = sb("inv_cnt", [P, JR, 16])
        vecs = sb("vecs", [P, V_N])
        taps = sb("taps", [P, CW * KD])
        spc = sb("spc", [P, JR])
        keyT = sb("keyT", [P, 4, P])
        poolw = sb("poolw", [P, JR, P])
        bda = sb("bda", [P, JR, P])
        bdx = sb("bdx", [P, JR, P])
        sm = sb("sm", [P, 24])
        x = sb("x", [P, 3, D])
        xT = [sb("xT_s", [P, KD, NS]), sb("xT_p", [P, KD, SEQ])]
        yT = [sb("yT_s", [P, KD, 2, NS]), sb("yT_p", [P, KD, 1, SEQ])]
        lnp = sb("lnp", [P, 2, 2, D])
        wr = sb("wr", [P, WSLOT, KD, WC])
        hlast_s = sb("hlast_s", [P, JR, DB])
        hlast_p = sb("hlast_p", [P, JR])
        bn = sb("bn", [P, 2, 6])
        mv = sb("mv", [P, 3, 8])
        so = sb("so", [P, SLOTS, HALF])
        qT = sb("qT", [P, 16, P])
        sc = sb("sc", [P, 16, NK])
        sc2 = sb("sc2", [P, NK])
        tv = sb("tv", [P, 16, TOPK])
        ti = sb("ti", [P, 16, TOPK], U32)
        tif = sb("tif", [P, 16, TOPK])
        cand = sb("cand", [P, HEADS, TOPK, TOPK])
        cand2 = sb("cand2", [P, TOPK * TOPK])
        oh = cand
        sv = sb("sv", [P, HEADS, TOPK])
        ci = sb("ci", [P, HEADS, TOPK], U32)
        cab = sb("cab", [P, 2, HEADS, TOPK], U32)
        cabf = sb("cabf", [P, 2, HEADS, TOPK])
        e12 = sb("e12", [P, 2, HEADS, TOPK])
        eidx = sb("eidx", [P, 3, NK], I32)
        gate = sb("gate", [P, 3, HEADS, TOPK])
        gsm = sb("gsm", [P, HEADS])
        actv = sb("actv", [P, 3, NK])
        acg = sb("acg", [P, NK])
        stg = sb("stg", [P, 2, RING], I32)
        ring = sb("ring", [P, RING, D])
        acc = sb("acc", [P, 2, D])
        facc = sb("facc", [P, D])
        rows_v, rows_dw, rows_key = ring[0:V_N, 0, 0:P], ring[0:124, 0, 128:384], ring[:, 1, 0:512]
        rows_sp, rows_sr, rows_sh = ring[0:DB * PB, 2, 0:HALF], ring[0:DB * RB, 3, 0:HALF], ring[0:DB, 4, 0:HALF]

        m0 = ExitStack()
        pp = sb("pp", [P, JR, PB + SEQ], stack=m0)
        ps_ = sb("ps", [P, JR, DB, PB + DS], stack=m0)
        rp = sb("rp", [P, JR, RB + SEQ], stack=m0)
        rs = sb("rs", [P, JR, DB, RB + DS], stack=m0)
        dps = sb("dps", [P, JR, DB * PB], stack=m0)
        drs = sb("drs", [P, JR, DB * RB], stack=m0)
        h0 = sb("h0", [P, JR, DB], stack=m0)
        wab = sb("wab", [P, 2, PB + SEQ], stack=m0)
        rnn = sb("rnn", [P, 6, 2, SEQ], stack=m0)
        m0.close()
        rnn_s = rnn[:].rearrange("p i j t -> p (i j t)")[:, 0:6 * JR * NS].rearrange("p (i j t) -> p i j t", i=6, j=JR)
        m1 = ExitStack()
        cp = sb("cp", [P, KD, CB + SEQ], stack=m1)
        cs = sb("cs", [P, KD, DB, CB + DS], stack=m1)
        sg = sb("sg", [P, 2, SEQ], stack=m1)
        sq = sb("sq", [P, KD * SEQ], stack=m1)
        mub = sb("mub", [P, SEQ], stack=m1)
        rsb = sb("rsb", [P, 3, SEQ], stack=m1)
        diag = sb("diag", [P, DIAG, P], stack=m1)
        m1.close()
        rows_sc = sq[0:120, 0:2 * D].rearrange("p (h c) -> p h c", h=2)
        dcs = sq[:, 0:KD * DB * CB].rearrange("p (f r) -> p f r", f=KD)

        pb = [ctx.enter_context(nc.psum_tensor(f"bank{b}", [P, 512], F32)) for b in range(8)]

        s_mm = sem("s_mm")
        s_moved = [sem(f"s_moved{b}") for b in range(8)]
        s_x = [sem(f"s_x{st}") for st in range(2)]
        s_vec = sem("s_vec")
        s_key = sem("s_key")
        s_st = sem("s_st")
        s_bd = sem("s_bd")
        s_scv = sem("s_scv")
        s_w = [sem(f"s_w{i}") for i in range(WSLOT)]
        s_ln = [sem(f"s_ln{i}") for i in range(2)]
        s_so = [sem(f"s_so{i}") for i in range(SLOTS)]
        s_out = sem("s_out")
        s_cst = sem("s_cst")
        s_bz = sem("s_bz")
        s_hist = sem("s_hist")
        s_dv = sem("s_dv")
        s_own = sem("s_own")
        s_inv = sem("s_inv")
        s_lam1 = sem("s_lam1")
        s_lam2 = sem("s_lam2")
        s_spc = sem("s_spc")
        s_rows = sem("s_rows")
        s_pooled = sem("s_pooled")
        s_xc = sem("s_xc")
        s_th = sem("s_th")
        s_q2 = sem("s_q2")
        s_rt = sem("s_rt")
        s_yb = sem("s_yb")
        s_var = sem("s_var")
        s_sd = sem("s_sd")
        s_xn = sem("s_xn")
        s_sub = sem("s_sub")
        s_ex = sem("s_ex")
        s_sel = sem("s_sel")
        s_e = sem("s_e")
        s_g = [sem(f"s_g{i}") for i in range(RING)]
        s_used = sem("s_used")
        s_turn = sem("s_turn")
        s_stg = sem("s_stg")
        s_act = sem("s_act")
        s_gel = sem("s_gel")
        s_facc = sem("s_facc")
        s_sig = sem("s_sig")
        s_glu = sem("s_glu")
        s_diag = sem("s_diag")
        s_cvf = sem("s_cvf")
        s_dcv = sem("s_dcv")
        s_cm = sem("s_cm")
        s_csq = sem("s_csq")
        s_cve = sem("s_cve")
        s_csd = sem("s_csd")
        s_cn = sem("s_cn")
        s_silu = sem("s_silu")

        def moved(eng, name):
            g = GID[name]
            eng.wait_ge(s_moved[g % 8], g // 8 + 1)

        def filled(eng, name):
            eng.wait_ge(s_mm, GID[name] + 1)
            return pb[GID[name] % 8], s_moved[GID[name] % 8]

        block = ctx.enter_context(nc.Block())

        @block.sync
        def _(sp):
            def rows_of_weights(name):
                return {"in": w_in_even[0], "out": w_out_even[0], "pw": w_pw[0]}[name]

            def weights(n0, n1):
                for i in range(n0, n1):
                    name, layer, c, _ = BLOCKS[i]
                    if i >= WSLOT:
                        sp.wait_ge(s_mm, GID[BLOCKS[i - WSLOT][3]] + 1)
                    slot = i % WSLOT
                    if name == "glu":
                        v = w_glu[0].rearrange("(k p) (a n) -> p a k n", p=P, a=2)
                        for a in range(2):
                            sp.dma_start(wr[:, slot, :, a * P:(a + 1) * P], v[:, a, :, c * P:(c + 1) * P]).then_inc(s_w[slot], 16)
                    else:
                        w = peer_wq[layer] if name == "q" else rows_of_weights(name)
                        sp.dma_start(wr[:, slot], w.rearrange("(k p) n -> p k n", p=P)[:, :, c * WC:(c + 1) * WC])\
                          .then_inc(s_w[slot], 16)

            for h in range(2):
                sp.dma_start(x[h * NS:(h + 1) * NS, 2, :], x_sample.rearrange("b s d -> (b s) d")).then_inc(s_x[S], 16)
            weights(0, WSLOT)
            for src, r0, r1 in ((rnn_conv_w[0].rearrange("w (j p) -> (w j) p", p=P), V_CW, V_CB),
                                (rnn_conv_b.rearrange("a (j p) -> (a j) p", p=P), V_CB, V_BA),
                                (rg_ba.rearrange("a (j p) -> (a j) p", p=P), V_BA, V_BX),
                                (rg_bx.rearrange("a (j p) -> (a j) p", p=P), V_BX, V_LAM),
                                (rg_lambda.rearrange("a (j p) -> (a j) p", p=P), V_LAM, V_PS),
                                (pool_scale.rearrange("a (j p) -> (a j) p", p=P), V_PS, V_DB),
                                (dw_b.rearrange("a (j p) -> (a j) p", p=P), V_DB, V_CG),
                                (conv_ln_g.rearrange("a (j p) -> (a j) p", p=P), V_CG, V_CBT),
                                (conv_ln_b.rearrange("a (j p) -> (a j) p", p=P), V_CBT, V_N)):
                sp.dma_start(rows_v[r0:r1, :], src).then_inc(s_vec, 16)
            dwr = dw_w[0].rearrange("w (f p) -> (w f) p", p=P)
            for h in range(2):
                sp.dma_start(rows_dw[:, h * P:(h + 1) * P], dwr[h * 124:(h + 1) * 124, :]).then_inc(s_vec, 16)
            for layer in range(2):
                for i, k in enumerate((peer_k1, peer_k2)):
                    sp.dma_start(rows_key[:, (2 * layer + i) * P:(2 * layer + i + 1) * P], k[layer]).then_inc(s_key, 16)
            sp.dma_start(rows_sp, state_pool[0].rearrange("b t c -> (b t) c")).then_inc(s_st, 16)
            sp.dma_start(rows_sr, state_rnn_conv[0].rearrange("b t c -> (b t) c")).then_inc(s_st, 16)
            sp.dma_start(rows_sh, state_rnn_h[0]).then_inc(s_st, 16)
            sp.dma_start(poolw[:], pool_w[0].rearrange("g c d -> c g d")).then_inc(s_bd, 16)
            sp.wait_ge(s_bz, 2)
            for dst, src in ((bda, rg_wa), (bdx, rg_wx)):
                v = src[0].rearrange("(j h) i o -> h i j o", h=2)
                for h in range(2):
                    sp.dma_start(dst[64 * h:64 * h + 64, :, 64 * h:64 * h + 64], v[h]).then_inc(s_bd, 16)
            for n in range(2):
                sp.dma_start(x[:, n, :], x_prompt[0, n * P:(n + 1) * P, :]).then_inc(s_x[Q], 16)

            def ln_rows(i):
                layer = i // 2
                for j, v in enumerate((ln_ffn_g, ln_ffn_b) if i % 2 else (ln_mix_g, ln_mix_b)):
                    sp.dma_start(lnp[:, i % 2, j, :], v[layer:layer + 1, :].to_broadcast([P, D])).then_inc(s_ln[i % 2], 16)

            ln_rows(0)
            ln_rows(1)
            n_s, n_q = 18, 26
            weights(WSLOT, n_s + n_q)
            sp.wait_ge(s_xn, NORMS.index((0, 1)) + 1)
            ln_rows(2)
            scr_ = state_conv[0].rearrange("b t c -> (b t) c")
            for p in range(2):
                sp.dma_start(rows_sc[:, p, :], scr_[120 * p:120 * p + 120, :]).then_inc(s_scv, 16)
            weights(n_s + n_q, n_s + n_q + 20 + WSLOT)
            sp.wait_ge(s_xn, NORMS.index((1, 1)) + 1)
            ln_rows(3)
            weights(n_s + n_q + 20 + WSLOT, len(BLOCKS))
            sp.wait_ge(s_xn, NORMS.index((3, 2)) + 1)
            sp.dma_start(y_sample.rearrange("b s d -> (b s) d"), x[0:NS, 2, :]).then_inc(s_out, 16)
            for n in range(2):
                sp.wait_ge(s_xn, NORMS.index((3, n)) + 1)
                sp.dma_start(y_prompt[0, n * P:(n + 1) * P, :], x[:, n, :]).then_inc(s_out, 16)
            sp.wait_ge(s_out, 48)
            for i in range(SLOTS):
                sp.wait_ge(s_so[i], 16 * 4)

        @block.tensor
        def _(pe):
            todo = list(GROUPS)
            block_no = [0]
            landed = [0] * WSLOT

            def begin(name):
                assert todo.pop(0) == name, name
                g = GID[name]
                if g >= 8:
                    pe.wait_ge(s_moved[g % 8], g // 8)
                return pb[g % 8]

            def next_block(name):
                i = block_no[0]
                block_no[0] += 1
                assert BLOCKS[i][0] == name
                landed[i % WSLOT] += 32 if name == "glu" else 16
                pe.wait_ge(s_w[i % WSLOT], landed[i % WSLOT])
                return wr[:, i % WSLOT]

            def project(out, w, rhs):
                for k in range(KD):
                    last = nc.tensor.matmul(out, w[:, k, :], rhs[:, k, :], start=(k == 0), stop=(k == KD - 1))
                return last

            def x_transposes(layer, part, tiles):
                for n in tiles:
                    if layer or part:
                        pe.wait_ge(s_xn, NORMS.index((2 * layer + part - 1, n)) + 1)
                    else:
                        pe.wait_ge(s_x[STREAM[n]], 32)
                    rows = width(n)
                    for q in range(2):
                        b = begin(("xT", layer, part, n, q))
                        for i in range(4):
                            f = 4 * q + i
                            last = nc.tensor.transpose(b[:, i * rows:(i + 1) * rows],
                                                       x[0:rows, n, f * P:(f + 1) * P], ident[0:rows, 0:rows])
                        last.then_inc(s_mm, 1)

            def project_out(layer, st):
                y = yT[st][:].rearrange("p k a t -> p k (a t)")
                for blk in range(D // WC):
                    w = next_block("pw" if layer else "out")
                    for n in TILES[st]:
                        b = begin(("o", layer, n, blk))
                        t0 = 0 if n == 2 else n * P
                        for k in range(KD):
                            last = nc.tensor.matmul(b[:, 0:WC], y[:, k, t0:t0 + P], w[:, k, :],
                                                    start=(k == 0), stop=(k == KD - 1))
                        last.then_inc(s_mm, 1)

            def front(layer, n):
                x_transposes(layer, 1, (n,))
                moved(pe, ("xT", layer, 1, n, 1))
                t0, w_ = (0, NS) if n == 2 else (n * P, P)
                rhs = xT[STREAM[n]][:, :, t0:t0 + w_]
                for c in range(4):
                    b = begin(("q", layer, n, c))
                    for i in range(4):
                        if i % 2 == 0:
                            w = next_block("q")
                        last = project(b[:, i * w_:(i + 1) * w_], w[:, :, (i % 2) * P:(i % 2 + 1) * P], rhs)
                    last.then_inc(s_mm, 1)
                moved(pe, ("q", layer, n, 3))
                for i in range(HEADS_OF[n] // 2):
                    b = begin(("s", layer, n, i))
                    for j in range(4):
                        f = 4 * i + j
                        last = nc.tensor.matmul(b[:, j * P:(j + 1) * P], qT[:, f, :], keyT[:, 2 * layer + f % 2, :],
                                                start=True, stop=True)
                    last.then_inc(s_mm, 1)

            def fold(layer):
                pe.wait_ge(s_cst, 7)
                pe.wait_ge(s_facc, layer + 1)
                for h in range(2):
                    b = begin(("fold", layer, h))
                    nc.tensor.matmul(b[:, :], foldm[:], facc[:, h * 512:(h + 1) * 512],
                                     start=True, stop=True).then_inc(s_mm, 1)

            def turn_states(name, srcs, rows):
                b = begin(name)
                for i, src in enumerate(srcs):
                    last = nc.tensor.transpose(b[0:rows, i * P:(i + 1) * P], src, ident[:])
                last.then_inc(s_mm, 1)

            def even_mixer(st):
                cols = COLS[st]
                x_transposes(0, 0, TILES[st])
                moved(pe, ("xT", 0, 0, TILES[st][-1], 1))
                for c in range(6):
                    w = next_block("in")
                    for i in range(2):
                        b = begin(("z0", st, 2 * c + i))
                        project(b[:, 0:cols], w[:, :, i * P:(i + 1) * P], xT[st]).then_inc(s_mm, 1)
                if st == S:
                    pe.wait_ge(s_rows, 2)
                else:
                    moved(pe, ("z0", st, 7))
                for k, (buf, rows) in enumerate(((dps, DB * PB), (drs, DB * RB)) if st == S else ((pp, PB), (rp, RB))):
                    turn_states(("st0", st, k), [buf[:, j, 0:] if st == S else buf[:, j, SEQ:] for j in range(JR)], rows)
                pe.wait_ge(s_bd, 16 * 5)
                for j in range(JR):
                    pe.wait_ge(s_pooled, st * JR + j + 1)
                    b = begin(("ya", st, j))
                    nc.tensor.matmul(b[:, 0:cols], poolw[:, j, :], yT[st][:, j, 0, :], start=True, stop=True).then_inc(s_mm, 1)
                for j in range(JR):
                    pe.wait_ge(s_xc, st * JR + j + 1)
                    xc = rnn[:, 0, j % 2, :] if st == Q else rnn_s[:, 0, j, :]
                    for w, m in (("ga", bda), ("gx", bdx)):
                        b = begin((w, st, j))
                        nc.tensor.matmul(b[:, 0:cols], m[:, j, :], xc, start=True, stop=True).then_inc(s_mm, 1)
                pe.wait_ge(s_yb, 1 if st == S else 3)
                if st == S:
                    turn_states(("h0", st), [hlast_s[:, j, :] for j in range(JR)], DB)
                else:
                    turn_states(("h0", st), [hlast_p[:, j:j + 1] for j in range(JR)], 1)
                moved(pe, ("ya", st, JR - 1))
                project_out(0, st)

            def odd_mixer(st):
                cols = COLS[st]
                x_transposes(1, 0, TILES[st])
                if st == S:
                    pe.wait_ge(s_scv, 32)
                    for p in range(2):
                        for q in range(2):
                            b = begin(("scv", p, q))
                            for i in range(4):
                                f = 4 * q + i
                                last = nc.tensor.transpose(b[:, i * 120:(i + 1) * 120], rows_sc[:, p, f * P:(f + 1) * P],
                                                           ident[0:120, 0:120])
                            last.then_inc(s_mm, 1)
                moved(pe, ("xT", 1, 0, TILES[st][-1], 1))
                for f in range(KD):
                    w = next_block("glu")
                    b = begin(("z1", st, f))
                    project(b[:, 0:cols], w[:, :, 0:P], xT[st])
                    project(b[:, 256:256 + cols], w[:, :, P:2 * P], xT[st]).then_inc(s_mm, 1)
                if st == S:
                    pe.wait_ge(s_rows, 3)
                    for k in range(4):
                        p, q = k // 2, k % 2
                        turn_states(("cst", st, k), [dcs[:, 4 * q + i, 120 * p:120 * p + 120] for i in range(4)], 120)
                else:
                    pe.wait_ge(s_glu, KD * (st + 1))
                    for k in range(2):
                        turn_states(("cst", st, k), [cp[:, 4 * k + i, SEQ:] for i in range(4)], CB)
                d = KD * CW * st
                for f in range(KD if st == S else PE_F):
                    b = begin(("cv", st, f))
                    for w in range(CW):
                        pe.wait_ge(s_diag, d + 1)
                        src = cs[:, f, :, w:w + DS] if st == S else cp[:, f, w:w + SEQ]
                        out = b[:, 0:cols].rearrange("p (b s) -> p b s", b=DB) if st == S else b[:, 0:cols]
                        last = nc.tensor.matmul(out, diag[:, d % DIAG, :], src, start=(w == 0), stop=(w == CW - 1))
                        if w < CW - 1:
                            last.then_inc(s_cvf, 1)
                        d += 1
                    last.then_inc(s_mm, 1)
                moved(pe, ("cv", st, (KD if st == S else PE_F) - 1))
                if st == Q:
                    pe.wait_ge(s_dcv, 1)
                b = begin(("mu", st))
                for f in range(KD):
                    last = nc.tensor.matmul(b[:, 0:cols], mean_m[:], yT[st][:, f, 0, :], start=(f == 0), stop=(f == KD - 1))
                last.then_inc(s_mm, 1)
                pe.wait_ge(s_csq, st + 1)
                b = begin(("var", st))
                for f in range(KD):
                    last = nc.tensor.matmul(b[:, 0:cols], mean_m[:], sq[:, f * cols:(f + 1) * cols],
                                            start=(f == 0), stop=(f == KD - 1))
                last.then_inc(s_mm, 1)
                pe.wait_ge(s_silu, KD * (st + 1))
                project_out(1, st)

            pe.wait_ge(s_cst, 5)
            pe.wait_ge(s_vec, 11 * 16)
            b = begin(("vec",))
            nc.tensor.transpose(b[:, 0:V_N], rows_v, ident[0:V_N, 0:V_N]).then_inc(s_mm, 1)
            for h in range(2):
                b = begin(("dw", h))
                nc.tensor.transpose(b[:, 0:124], rows_dw[:, h * P:(h + 1) * P], ident[0:124, 0:124]).then_inc(s_mm, 1)
            pe.wait_ge(s_key, 64)
            b = begin(("key",))
            for i in range(4):
                last = nc.tensor.transpose(b[:, i * P:(i + 1) * P], rows_key[:, i * P:(i + 1) * P], ident[:])
            last.then_inc(s_mm, 1)
            pe.wait_ge(s_st, 48)
            b = begin(("stp",))
            for j in range(JR):
                last = nc.tensor.transpose(b[:, j * 120:(j + 1) * 120], rows_sp[:, j * P:(j + 1) * P], ident[0:120, 0:120])
            last.then_inc(s_mm, 1)
            b = begin(("srh",))
            for j in range(JR):
                nc.tensor.transpose(b[:, j * 24:(j + 1) * 24], rows_sr[:, j * P:(j + 1) * P], ident[0:24, 0:24])
            for j in range(JR):
                last = nc.tensor.transpose(b[:, 96 + j * 8:104 + j * 8], rows_sh[:, j * P:(j + 1) * P], ident[0:8, 0:8])
            last.then_inc(s_mm, 1)
            for layer, mixer in ((0, even_mixer), (1, odd_mixer)):
                mixer(S)
                front(layer, 2)
                mixer(Q)
                front(layer, 0)
                front(layer, 1)
                fold(layer)
            assert not todo and block_no[0] == len(BLOCKS)

        @block.scalar
        def _(act):
            A = nc.scalar.activation
            n_out = [0]
            n_diag = [0]

            def store_rows(name, rows, dst):
                k = n_out[0]
                n_out[0] += 1
                if k >= SLOTS:
                    act.wait_ge(s_so[k % SLOTS], 16 * (k // SLOTS))
                b, free = filled(act, name)
                A(so[0:rows, k % SLOTS, :], b[0:rows, :], ACT.Copy).then_inc(free, 1)
                moved(act, name)
                act.dma_start(dst, so[0:rows, k % SLOTS, :]).then_inc(s_so[k % SLOTS], 16)

            def x_columns(layer, part, tiles):
                for n in tiles:
                    cols = width(n)
                    t0 = 0 if n == 2 else n * P
                    for q in range(2):
                        b, free = filled(act, ("xT", layer, part, n, q))
                        A(xT[STREAM[n]][:, 4 * q:4 * q + 4, t0:t0 + cols],
                          b[:, 0:4 * cols].rearrange("p (f t) -> p f t", f=4), ACT.Copy).then_inc(free, 1)

            def root(i, n):
                act.wait_ge(s_var, NORMS.index((i, n)) + 1)
                A(mv[:, n, 3:4], mv[:, n, 2:3], ACT.Sqrt).then_inc(s_sd, 1)

            def front(layer, n):
                x_columns(layer, 1, (n,))
                w_ = width(n)
                c0 = CHOICES.index((layer, n))
                for c in range(4):
                    b, free = filled(act, ("q", layer, n, c))
                    src = b[:, 0:4 * w_].rearrange("p (f t) -> p f t", f=4)
                    if n < 2:
                        A(qT[:, 4 * c:4 * c + 4, :], src, ACT.Copy).then_inc(free, 1)
                    else:
                        A(qT[:, 4 * (c % 2):4 * (c % 2) + 4, (c // 2) * NS:(c // 2 + 1) * NS], src, ACT.Copy).then_inc(free, 1)
                if c0:
                    act.wait_ge(s_sel, c0)
                for i in range(HEADS_OF[n] // 2):
                    b, free = filled(act, ("s", layer, n, i))
                    A(sc[:, 4 * i:4 * i + 4, :].rearrange("p a k -> p (a k)"), b[:], ACT.Copy).then_inc(free, 1)

            def exps(layer, n):
                heads = HEADS_OF[n]
                act.wait_ge(s_sub, CHOICES.index((layer, n)) + 1)
                A(gate[:, n, 0:heads, :], gate[:, n, 0:heads, :], ACT.Exp).then_inc(s_ex, 1)

            def gelus(layer, n):
                k = [(l, m) for l, t, m, _, _ in PHASES if t == "u"].index((layer, n))
                act.wait_ge(s_act, k + 1)
                slots = HEADS_OF[n] * TOPK
                A(acg[:, 0:slots], actv[:, n, 0:slots], ACT.Gelu_apprx_tanh).then_inc(s_gel, 1)

            def even_mixer(st, meanwhile=None):
                cols = COLS[st]
                x_columns(0, 0, TILES[st])
                for ft in range(12):
                    b, free = filled(act, ("z0", st, ft))
                    if ft < 8:
                        j = ft % 4
                        if st == Q:
                            dst = (pp, rp)[ft // 4][:, j, (PB, RB)[ft // 4]:]
                            src = b[:, 0:cols]
                        else:
                            dst = (ps_, rs)[ft // 4][:, j, :, (PB, RB)[ft // 4]:]
                            src = b[:, 0:cols].rearrange("p (b s) -> p b s", b=DB)
                        A(dst, src, ACT.Copy).then_inc(free, 1)
                    else:
                        A(yT[st][:, JR + ft - 8, 0, :], b[:, 0:cols], ACT.Gelu_apprx_tanh).then_inc(free, 1)
                if st == S:
                    moved(act, ("z0", S, 7))
                    for dst, src in ((dps, ps_), (drs, rs)):
                        for j in range(JR):
                            last = A(dst[:, j, :].rearrange("p (b t) -> p b t", b=DB), src[:, j, :, DS:], ACT.Copy)
                        last.then_inc(s_rows, 1)
                if meanwhile:
                    meanwhile()
                outs = ((o_pool_s, DB * PB), (o_rconv_s, DB * RB)) if st == S else ((o_pool_p, PB), (o_rconv_p, RB))
                for k, (dst, rows) in enumerate(outs):
                    store_rows(("st0", st, k), rows, dst[0].rearrange("b t c -> (b t) c"))
                for j in range(JR):
                    b, free = filled(act, ("ya", st, j))
                    copies = 2 if st == S else 1
                    A(yT[st][:, j], b[:, 0:cols].unsqueeze(1).to_broadcast([P, copies, cols]), ACT.Identity,
                      scale=vecs[:, V_PS + j:V_PS + j + 1]).then_inc(free, 1)
                if st == S:
                    act.wait_ge(s_spc, 1)
                jb = JR if st == S else 2
                for j0 in range(0, JR, jb):
                    buf = rnn_s if st == S else rnn
                    for j in range(j0, j0 + jb):
                        for w, i, v in (("ga", 1, V_BA), ("gx", 2, V_BX)):
                            b, free = filled(act, (w, st, j))
                            if j0 and j == j0 and i == 1:
                                act.wait_ge(s_yb, 2)
                            A(buf[:, i, j - j0, :], b[:, 0:cols], ACT.Sigmoid, bias=vecs[:, v + j:v + j + 1]).then_inc(free, 1)
                    moved(act, ("gx", st, j0 + jb - 1))
                    for j in range(j0, j0 + jb):
                        A(buf[:, 3, j - j0, :], buf[:, 1, j - j0, :], ACT.Tanh, scale=spc[:, j:j + 1]).then_inc(s_th, 1)
                    act.wait_ge(s_q2, 1 if st == S else 2 + j0 // jb)
                    A(buf[:, 3], buf[:, 1], ACT.Sqrt).then_inc(s_rt, 1)
                store_rows(("h0", st), DB if st == S else 1, (o_h_s if st == S else o_h_p)[0])
                for n in TILES[st]:
                    root(0, n)

            def odd_mixer(st, meanwhile):
                cols = COLS[st]
                x_columns(1, 0, TILES[st])
                if st == S:
                    for p in range(2):
                        for q in range(2):
                            b, free = filled(act, ("scv", p, q))
                            for i in range(4):
                                last = A(cs[:, 4 * q + i, 4 * p:4 * p + 4, 0:CB],
                                         b[:, 120 * i:120 * i + 120].rearrange("p (b t) -> p b t", b=4), ACT.Copy)
                            last.then_inc(free, 1)
                for f in range(KD):
                    b, _ = filled(act, ("z1", st, f))
                    k = KD * st + f
                    if k >= 2:
                        act.wait_ge(s_glu, k - 1)
                    A(sg[:, f % 2, 0:cols], b[:, 256:256 + cols], ACT.Sigmoid).then_inc(s_sig, 1)
                if st == S:
                    act.wait_ge(s_glu, KD)
                    moved(act, ("scv", 1, 1))
                    for f in range(KD):
                        last = A(dcs[:, f, :].rearrange("p (b t) -> p b t", b=DB), cs[:, f, :, DS:], ACT.Copy)
                    last.then_inc(s_rows, 1)
                    outs = [(120, o_conv_s[0].rearrange("b t c -> (b t) c")[120 * p:120 * p + 120, q * HALF:(q + 1) * HALF])
                            for p in range(2) for q in range(2)]
                else:
                    outs = [(CB, o_conv_p[0, 0, :, q * HALF:(q + 1) * HALF]) for q in range(2)]
                    meanwhile()
                for k, (rows, dst) in enumerate(outs):
                    store_rows(("cst", st, k), rows, dst)
                for f in range(KD if st == S else PE_F):
                    for w in range(CW):
                        d = n_diag[0]
                        n_diag[0] += 1
                        if d >= DIAG:
                            g, t = divmod(d - DIAG, CW)
                            name = ("cv", S, g) if g < KD else ("cv", Q, g - KD)
                            if t == CW - 1:
                                act.wait_ge(s_mm, GID[name] + 1)
                            else:
                                act.wait_ge(s_cvf, (d - DIAG) - g + 1)
                        A(diag[:, d % DIAG, :], ident[:], ACT.Copy, scale=taps[:, w * KD + f:w * KD + f + 1]).then_inc(s_diag, 1)
                    if f:
                        conv_out(st, f - 1)
                conv_out(st, (KD if st == S else PE_F) - 1)
                if st == S:
                    meanwhile()
                b, free = filled(act, ("mu", st))
                A(mub[:, 0:cols], b[:, 0:cols], ACT.Copy).then_inc(free, 1)
                y = yT[st][:, :, 0, :]
                act.wait_ge(s_cm, st + 1)
                A(sq[:, 0:KD * cols].rearrange("p (f t) -> p f t", f=KD), y, ACT.Square).then_inc(s_csq, 1)
                act.wait_ge(s_cve, st + 1)
                A(rsb[:, 1, 0:cols], rsb[:, 0, 0:cols], ACT.Sqrt).then_inc(s_csd, 1)
                act.wait_ge(s_cn, st + 1)
                for f in range(KD):
                    copies = 2 if st == S else 1
                    src = rsb_y(st, f)
                    A(yT[st][:, f], src.unsqueeze(1).to_broadcast([P, copies, cols]), ACT.Silu,
                      bias=vecs[:, V_CBT + f:V_CBT + f + 1], scale=vecs[:, V_CG + f:V_CG + f + 1]).then_inc(s_silu, 1)
                for n in TILES[st]:
                    root(2, n)

            def rsb_y(st, f):
                cols = COLS[st]
                return sq[:, f * cols:(f + 1) * cols]

            def conv_out(st, f):
                b, free = filled(act, ("cv", st, f))
                A(yT[st][:, f, 0, :], b[:, 0:COLS[st]], ACT.Identity, bias=vecs[:, V_DB + f:V_DB + f + 1]).then_inc(free, 1)

            b, free = filled(act, ("vec",))
            A(vecs[:], b[:, 0:V_N], ACT.Copy).then_inc(free, 1)
            for h in range(2):
                b, free = filled(act, ("dw", h))
                A(taps[:, h * 124:(h + 1) * 124], b[:, 0:124], ACT.Copy).then_inc(free, 1)
            b, free = filled(act, ("key",))
            A(keyT[:].rearrange("p a k -> p (a k)"), b[:], ACT.Copy).then_inc(free, 1)
            b, free = filled(act, ("stp",))
            A(ps_[:, :, :, 0:PB], b[:, 0:480].rearrange("p (j b t) -> p j b t", j=JR, b=DB), ACT.Copy).then_inc(free, 1)
            b, free = filled(act, ("srh",))
            A(rs[:, :, :, 0:RB], b[:, 0:96].rearrange("p (j b t) -> p j b t", j=JR, b=DB), ACT.Copy)
            A(h0[:], b[:, 96:128].rearrange("p (j b) -> p j b", j=JR), ACT.Copy).then_inc(free, 1)
            act.wait_ge(s_lam1, 1)
            A(sm[:, 4:8], sm[:, 0:4], ACT.Exp).then_inc(s_lam2, 1)

            even_mixer(S)
            front(0, 2)
            exps(0, 2)
            even_mixer(Q, lambda: gelus(0, 2))
            front(0, 0)
            exps(0, 0)
            front(0, 1)
            exps(0, 1)
            gelus(0, 0)
            root(1, 2)
            odd_mixer(S, lambda: gelus(0, 1))
            front(1, 2)
            exps(1, 2)
            root(1, 0)
            root(1, 1)
            odd_mixer(Q, lambda: gelus(1, 2))
            front(1, 0)
            exps(1, 0)
            front(1, 1)
            exps(1, 1)
            gelus(1, 0)
            root(3, 2)
            gelus(1, 1)
            root(3, 0)
            root(3, 1)

        @block.vector
        def _(dve):
            V = nc.vector
            count = {}

            def step(ins, s=s_dv):
                count[s.name] = count.get(s.name, 0) + 1
                ins.then_inc(s, 1)
                dve.wait_ge(s, count[s.name])

            used = [0]

            def use_row(tab, n, k, col):
                if tab == "u":
                    V.scalar_tensor_tensor(acc[:, k % 2, :], ring[:, k, :], 1.0, x[:, n, :], ALU.mult, ALU.mult,
                                           accum_out=actv[:, n, col]).then_inc(s_used, 1)
                else:
                    V.scalar_tensor_tensor(acc[:, k % 2, :], ring[:, k, :], actv[:, n, col], acc[:, k % 2, :],
                                           ALU.mult, ALU.add).then_inc(s_used, 1)

            def phase_of(at):
                return next(p for p in PHASES if p[4] <= at < p[4] + p[3])

            def enter(at):
                layer, tab, n, slots, start = phase_of(at)
                if tab == "v" and at == start:
                    step(V.memset(acc[:], 0.0))

            def leave(at):
                layer, tab, n, slots, start = phase_of(at - 1)
                if at != start + slots:
                    return
                dve.wait_ge(s_used, RING + at)
                if tab == "u":
                    k = [(l, m) for l, t, m, _, _ in PHASES if t == "u"].index((layer, n))
                    dve.sem_inc(s_act, 1)
                    dve.wait_ge(s_gel, k + 1)
                    step(V.tensor_tensor(actv[:, n, 0:slots], acg[:, 0:slots],
                                         gate[:, n].rearrange("p h k -> p (h k)")[:, 0:slots], ALU.mult))
                elif n == 2:
                    step(V.tensor_tensor(facc[:], acc[:, 0, :], acc[:, 1, :], ALU.add), s_facc)
                else:
                    step(V.scalar_tensor_tensor(x[:, n, :], x[:, n, :], ALPHA, acc[:, 0, :], ALU.mult, ALU.add))
                    step(V.tensor_tensor(x[:, n, :], x[:, n, :], acc[:, 1, :], ALU.add))

            def rows(batches=1):
                for _ in range(batches):
                    at = used[0]
                    enter(at)
                    _, tab, n, _, start = phase_of(at)
                    for k in range(RING):
                        dve.wait_ge(s_g[k], 16 * (at // RING + 1))
                        dve.wait_ge(s_used, RING + at + k - 1)
                        col = at - start + k
                        use_row(tab, n, k, slice(col, col + 1))
                    used[0] += RING
                    leave(used[0])

            def rest_of_phase():
                at = used[0]
                _, tab, n, slots, start = phase_of(at)
                enter(at)
                left = start + slots - at
                assert left
                with dve.Fori(0, left // RING) as i:
                    for k in range(RING):
                        dve.wait_ge(s_g[k], i * 16 + (at // RING + 1) * 16)
                        dve.wait_ge(s_used, i * RING + (RING + at + k - 1))
                        use_row(tab, n, k, bass.ds(i * RING + (at - start + k), 1))
                used[0] += left
                leave(used[0])

            def upto(phase):
                def some(batches=1):
                    for _ in range(batches):
                        if used[0] < next(p[4] + p[3] for p in PHASES if p[:3] == phase):
                            rows()
                return some

            def nothing(batches=1):
                pass

            def inverse(root, var, r, t):
                step(V.reciprocal(r, root))
                step(V.tensor_tensor(t, r, r, ALU.mult))
                step(V.tensor_tensor(t, t, var, ALU.mult))
                step(V.tensor_scalar(t, t, -0.5, 1.5, ALU.mult, ALU.add))
                step(V.tensor_tensor(r, r, t, ALU.mult))

            def layer_norm(i, n):
                layer = i // 2
                dve.wait_ge(s_ln[i % 2], 32 * (i // 2 + 1))
                if i % 2 == 0:
                    pieces = [(("o", layer, n, blk), WC) for blk in range(D // WC)]
                elif n == 2:
                    pieces = [(("fold", layer, h), 512) for h in range(2)]
                else:
                    pieces = []
                for k, (name, w) in enumerate(pieces):
                    b, free = filled(dve, name)
                    xs = x[:, n, k * w:(k + 1) * w]
                    V.scalar_tensor_tensor(xs, xs, ALPHA, b[:, 0:w], ALU.mult, ALU.add).then_inc(free, 1)
                for name, _ in pieces:
                    moved(dve, name)
                for h in range(2):
                    last = V.bn_stats(bn[:, h, :], x[:, n, h * 512:(h + 1) * 512])
                    step(last)
                step(V.bn_aggr(mv[:, n, 0:2], bn[:].rearrange("p h c -> p (h c)")))
                step(V.tensor_scalar(mv[:, n, 2:3], mv[:, n, 1:2], EPS, None, ALU.add), s_var)
                dve.wait_ge(s_sd, NORMS.index((i, n)) + 1)
                inverse(mv[:, n, 3:4], mv[:, n, 2:3], mv[:, n, 4:5], mv[:, n, 5:6])
                step(V.tensor_scalar(x[:, n, :], x[:, n, :], mv[:, n, 0:1], mv[:, n, 4:5], ALU.subtract, ALU.mult))
                step(V.tensor_tensor(x[:, n, :], x[:, n, :], lnp[:, i % 2, 0, :], ALU.mult))
                step(V.tensor_tensor(x[:, n, :], x[:, n, :], lnp[:, i % 2, 1, :], ALU.add), s_xn)

            def top16(vals, idx, src, spare):
                step(V.max(vals[:, 0:8], src))
                V.max_index(idx[:, 0:8], vals[:, 0:8], src).then_inc(s_dv, 1)
                count[s_dv.name] += 1
                step(V.match_replace(spare, vals[:, 0:8], src, -3.0e38))
                step(V.max(vals[:, 8:16], spare))
                step(V.max_index(idx[:, 8:16], vals[:, 8:16], spare))

            def choose(layer, n, between=nothing):
                heads = HEADS_OF[n]
                c = CHOICES.index((layer, n))
                for f in range(2 * heads):
                    moved(dve, ("s", layer, n, f // 4))
                    top16(tv[:, f, :], ti[:, f, :], sc[:, f, :], sc2[:])
                    if f % 2:
                        between()
                dve.sem_inc(s_sel, 1)
                g = 2 * heads
                step(V.tensor_copy(tif[:, 0:g, :], ti[:, 0:g, :]))
                v1 = tv[:, 0:g:2, :].unsqueeze(3).to_broadcast([P, heads, TOPK, TOPK])
                v2 = tv[:, 1:g:2, :].unsqueeze(2).to_broadcast([P, heads, TOPK, TOPK])
                step(V.tensor_tensor(cand[:, 0:heads], v1, v2, ALU.add))
                for h in range(heads):
                    top16(sv[:, h, :], ci[:, h, :], cand[:, h].rearrange("p a b -> p (a b)"), cand2[:])
                    if h % 2:
                        between()
                step(V.tensor_tensor(gate[:, n, 0:heads, :], sv[:, 0:heads, :],
                                     sv[:, 0:heads, 0:1].to_broadcast([P, heads, TOPK]), ALU.subtract), s_sub)
                step(V.tensor_single_scalar(cab[:, 0, 0:heads, :], ci[:, 0:heads, :], 4, ALU.logical_shift_right))
                step(V.tensor_single_scalar(cab[:, 1, 0:heads, :], ci[:, 0:heads, :], 15, ALU.bitwise_and))
                step(V.tensor_copy(cabf[:, :, 0:heads, :], cab[:, :, 0:heads, :]))
                for a in range(2):
                    o = oh[:, 0:heads]
                    step(V.tensor_tensor(o, cabf[:, a, 0:heads, :].unsqueeze(3).to_broadcast([P, heads, TOPK, TOPK]),
                                         iota_f[:].unsqueeze(1).unsqueeze(1).to_broadcast([P, heads, TOPK, TOPK]),
                                         ALU.is_equal))
                    step(V.tensor_tensor(o, o, tif[:, a:g:2, :].unsqueeze(2).to_broadcast([P, heads, TOPK, TOPK]), ALU.mult))
                    step(V.tensor_reduce(e12[:, a, 0:heads, :], o, AX.X, ALU.add))
                    between()
                step(V.tensor_scalar(e12[:, 0, 0:heads, :], e12[:, 0, 0:heads, :], float(NK), float(layer * NE),
                                     ALU.mult, ALU.add))
                step(V.tensor_tensor(eidx[:, n, 0:heads * TOPK].rearrange("p (h k) -> p h k", h=heads),
                                     e12[:, 0, 0:heads, :], e12[:, 1, 0:heads, :], ALU.add), s_e)
                dve.wait_ge(s_ex, c + 1)
                step(V.tensor_reduce(gsm[:, 0:heads], gate[:, n, 0:heads, :], AX.X, ALU.add))
                step(V.reciprocal(gsm[:, 0:heads], gsm[:, 0:heads]))
                step(V.tensor_tensor(gate[:, n, 0:heads, :], gate[:, n, 0:heads, :],
                                     gsm[:, 0:heads].unsqueeze(2).to_broadcast([P, heads, TOPK]), ALU.mult))

            def even_mixer(st, between=nothing):
                cols = COLS[st]
                if st == S:
                    moved(dve, ("stp",))
                for j in range(JR):
                    moved(dve, ("z0", st, j))
                    w = 2 << j
                    if st == Q:
                        src, tmp, end = pp[:, j, :], [wab[:, i, :] for i in range(2)], PB + SEQ
                    else:
                        src, end = ps_[:, j], PB + DS
                        tmp = [wab[:, i, 0:DB * end].rearrange("p (b t) -> p b t", b=DB) for i in range(2)]
                    tok = src[..., PB:]
                    for lev in range(j + 1):
                        d, lo = 1 << lev, (2 << lev) - 1
                        dst = tmp[lev % 2]
                        step(V.tensor_tensor(dst[..., lo:end], src[..., lo:end], src[..., lo - d:end - d], ALU.add))
                        src = dst
                    if st == Q:
                        step(V.tensor_tensor(yT[Q][:, j, 0, 0:16], src[:, PB:PB + 16], inv_cnt[:, j, :], ALU.mult))
                        step(V.tensor_tensor(yT[Q][:, j, 0, 0:16], yT[Q][:, j, 0, 0:16], tok[:, 0:16], ALU.subtract))
                        step(V.scalar_tensor_tensor(yT[Q][:, j, 0, 16:], src[:, PB + 16:], 1.0 / w, tok[:, 16:],
                                                    ALU.mult, ALU.subtract), s_pooled)
                    else:
                        step(V.scalar_tensor_tensor(yT[S][:, j, 0, :].rearrange("p (b s) -> p b s", b=DB), src[..., PB:end],
                                                    1.0 / w, tok, ALU.mult, ALU.subtract), s_pooled)
                    if j % 2:
                        between()
                jb = JR if st == S else 2
                buf = rnn_s if st == S else rnn
                moved(dve, ("srh",))
                dve.wait_ge(s_bz, 4)
                for j0 in range(0, JR, jb):
                    for j in range(j0, j0 + jb):
                        moved(dve, ("z0", st, 4 + j))
                        bias = vecs[:, V_CB + j:V_CB + j + 1]
                        tap = [vecs[:, V_CW + 4 * w + j:V_CW + 4 * w + j + 1] for w in range(4)]
                        dst = buf[:, 0, j - j0, :]
                        src = rp[:, j, :] if st == Q else rs[:, j]
                        if st == S:
                            dst = dst.rearrange("p (b s) -> p b s", b=DB)
                        n_ = SEQ if st == Q else DS
                        step(V.tensor_scalar(dst, src[..., 0:n_], tap[0], bias, ALU.mult, ALU.add))
                        for w in range(1, 4):
                            step(V.scalar_tensor_tensor(dst, src[..., w:w + n_], tap[w], dst, ALU.mult, ALU.add),
                                 s_xc if w == 3 else s_dv)
                    between()
                    xc, rg, ig, th, uv, av = [buf[:, i] for i in range(6)]
                    dve.wait_ge(s_th, JR * st + j0 + jb)
                    step(V.tensor_scalar(uv, th, 1.0, None, ALU.add))
                    step(V.reciprocal(uv, uv))
                    step(V.scalar_tensor_tensor(th, th, 2.0, uv, ALU.mult, ALU.mult))
                    step(V.tensor_scalar(av, th, -1.0, 1.0, ALU.mult, ALU.add))
                    step(V.tensor_scalar(uv, th, -1.0, 2.0, ALU.mult, ALU.add))
                    step(V.tensor_tensor(rg, th, uv, ALU.mult), s_q2)
                    step(V.tensor_tensor(ig, ig, xc, ALU.mult))
                    dve.wait_ge(s_rt, 1 if st == S else 2 + j0 // jb)
                    step(V.tensor_tensor(uv, th, ig, ALU.mult))
                    if st == S:
                        ap, up = [t.rearrange("p j (b s) -> p j b s", b=DB)[:, :, :, 0] for t in (av, uv)]
                        step(V.tensor_tensor(h0[:], h0[:], ap, ALU.mult))
                        step(V.tensor_tensor(up, up, h0[:], ALU.add))
                        step(V.memset(ap, 0.0))
                    for j in range(jb):
                        step(V.tensor_tensor_scan(xc[:, j, :], av[:, j, :], uv[:, j, :], 0.0, ALU.mult, ALU.add))
                    if st == S:
                        step(V.tensor_copy(hlast_s[:], xc[:, :, DS - 1:NS:DS]))
                    else:
                        step(V.tensor_copy(hlast_p[:, j0:j0 + jb], xc[:, :, SEQ - 1]))
                    moved(dve, ("z0", st, 11))
                    y = yT[st][:, JR + j0:JR + j0 + jb]
                    if st == S:
                        step(V.tensor_tensor(y[:, :, 1, :], xc, y[:, :, 0, :], ALU.mult))
                        step(V.tensor_copy(y[:, :, 0, :], y[:, :, 1, :]), s_yb)
                    else:
                        step(V.tensor_tensor(y[:, :, 0, :], xc, y[:, :, 0, :], ALU.mult), s_yb)
                    between()

            def odd_mixer(st, between, after_glu=None):
                cols = COLS[st]
                dve.wait_ge(s_hist, 1)
                for f in range(KD):
                    b, free = filled(dve, ("z1", st, f))
                    dve.wait_ge(s_sig, KD * st + f + 1)
                    dst, val, gt = cp[:, f, CB:], b[:, 0:cols], sg[:, f % 2, 0:cols]
                    if st == S:
                        dst = cs[:, f, :, CB:]
                        val, gt = [t.rearrange("p (b s) -> p b s", b=DB) for t in (val, gt)]
                    V.tensor_tensor(dst, val, gt, ALU.mult).then_inc(free, 1)
                    moved(dve, ("z1", st, f))
                    dve.sem_inc(s_glu, 1)
                    if f % 2:
                        between()
                if after_glu:
                    after_glu()
                y = yT[st][:, :, 0, :]
                if st == Q:
                    for f in range(PE_F, KD):
                        tap = [taps[:, w * KD + f:w * KD + f + 1] for w in range(CW)]
                        step(V.tensor_scalar(y[:, f, :], cp[:, f, 0:SEQ], tap[0], vecs[:, V_DB + f:V_DB + f + 1],
                                             ALU.mult, ALU.add))
                        for w in range(1, CW):
                            step(V.scalar_tensor_tensor(y[:, f, :], cp[:, f, w:w + SEQ], tap[w], y[:, f, :], ALU.mult, ALU.add))
                            if w % 10 == 0:
                                between()
                    dve.sem_inc(s_dcv, 1)
                moved(dve, ("mu", st))
                step(V.tensor_tensor(y, y, mub[:, 0:cols].unsqueeze(1).to_broadcast([P, KD, cols]), ALU.subtract), s_cm)
                b, free = filled(dve, ("var", st))
                V.tensor_scalar(rsb[:, 0, 0:cols], b[:, 0:cols], EPS, None, ALU.add).then_inc(free, 1)
                moved(dve, ("var", st))
                dve.sem_inc(s_cve, 1)
                dve.wait_ge(s_csd, st + 1)
                r = [rsb[:, i, 0:cols] for i in range(3)]
                inverse(r[1], r[0], r[2], mub[:, 0:cols])
                step(V.tensor_tensor(sq[:, 0:KD * cols].rearrange("p (f t) -> p f t", f=KD), y,
                                     r[2].unsqueeze(1).to_broadcast([P, KD, cols]), ALU.mult), s_cn)
                between()

            dve.sem_inc(s_used, RING)
            dve.wait_ge(s_cst, 6)
            step(V.tensor_copy(iota_f[:], iota_i[:]))
            for j in range(JR):
                step(V.tensor_scalar(inv_cnt[:, j, :], iota_f[:], 1.0, float(2 << j), ALU.add, ALU.min))
            step(V.reciprocal(inv_cnt[:], inv_cnt[:]))
            moved(dve, ("vec",))
            lam = vecs[:, V_LAM:V_LAM + JR]
            step(V.tensor_scalar(sm[:, 8:12], lam, -1.0, None, ALU.mult))
            step(V.tensor_tensor(sm[:, 0:4], sm[:, 8:12], lam, ALU.min), s_lam1)
            dve.wait_ge(s_lam2, 1)
            e, z, s2, p = sm[:, 4:8], sm[:, 12:16], sm[:, 16:20], sm[:, 20:24]
            step(V.tensor_scalar(z, e, 2.0, None, ALU.add))
            step(V.reciprocal(z, z))
            step(V.tensor_tensor(z, z, e, ALU.mult))
            step(V.tensor_tensor(s2, z, z, ALU.mult))
            step(V.tensor_scalar(p, s2, 1.0 / 17, None, ALU.mult))
            for c in (15, 13, 11, 9, 7, 5, 3):
                step(V.scalar_tensor_tensor(p, p, 1.0 / c, s2, ALU.add, ALU.mult))
            step(V.scalar_tensor_tensor(p, p, 1.0, z, ALU.add, ALU.mult))
            step(V.tensor_scalar(sm[:, 8:12], sm[:, 8:12], 0.0, 4.0, ALU.max, ALU.mult))
            step(V.scalar_tensor_tensor(spc[:], p, 8.0, sm[:, 8:12], ALU.mult, ALU.add), s_spc)

            even_mixer(S)
            layer_norm(0, 2)
            choose(0, 2)
            rows(6)
            even_mixer(Q, rows)
            rows(2)
            for n in TILES[Q]:
                layer_norm(0, n)
            rows(1)
            choose(0, 0, upto((0, "v", 2)))
            upto((0, "v", 2))(16)
            choose(0, 1, rows)
            rest_of_phase()
            layer_norm(1, 2)
            rows(4)
            odd_mixer(S, rows, rest_of_phase)
            layer_norm(2, 2)
            rows(4)
            choose(1, 2, upto((0, "v", 0)))
            rest_of_phase()
            layer_norm(1, 0)
            rest_of_phase()
            layer_norm(1, 1)
            rows(3)
            odd_mixer(Q, upto((1, "v", 2)), None)
            upto((1, "v", 2))(1)
            for n in TILES[Q]:
                layer_norm(2, n)
            upto((1, "v", 2))(1)
            choose(1, 0, upto((1, "v", 2)))
            upto((1, "v", 2))(16)
            choose(1, 1, rows)
            rest_of_phase()
            layer_norm(3, 2)
            rest_of_phase()
            rest_of_phase()
            layer_norm(3, 0)
            rest_of_phase()
            layer_norm(3, 1)
            assert used[0] == PHASES[-1][4] + PHASES[-1][3]

        @block.gpsimd
        def _(pool):
            G = nc.gpsimd
            G.memset(ident[:], 0.0).then_inc(s_cst, 1)
            G.memset(foldm[:], 0.0).then_inc(s_cst, 1)
            G.memset(mean_m[:], 1.0 / D).then_inc(s_cst, 1)
            pool.wait_ge(s_cst, 2)
            G.affine_select(out=ident[:], in_=ident[:], compare_op=ALU.not_equal, fill=1.0, base=0,
                            pattern=[[-1, P]], channel_multiplier=1).then_inc(s_cst, 1)
            f = foldm[:].rearrange("p (h q) -> p h q", h=2)
            G.affine_select(out=f, in_=f, compare_op=ALU.not_equal, fill=1.0, base=0,
                            pattern=[[0, 2], [-1, NS]], channel_multiplier=1).then_inc(s_cst, 1)
            pool.wait_ge(s_cst, 5)
            G.iota(iota_i[:], pattern=[[1, 16]], base=0, channel_multiplier=0).then_inc(s_cst, 1)
            G.affine_select(out=f, in_=f, compare_op=ALU.not_equal, fill=1.0, base=-NS,
                            pattern=[[0, 2], [-1, NS]], channel_multiplier=1).then_inc(s_cst, 1)
            G.memset(bda[:], 0.0).then_inc(s_bz, 1)
            G.memset(bdx[:], 0.0).then_inc(s_bz, 1)
            G.memset(pp[:, :, 0:PB], 0.0).then_inc(s_bz, 1)
            G.memset(rp[:, :, 0:RB], 0.0).then_inc(s_bz, 1)

            tables = {"u": peer_u.rearrange("l e d -> (l e) d"), "v": peer_v.rearrange("l e d -> (l e) d")}
            for layer, tab, n, slots, start in PHASES:
                if (layer, tab, n) == (0, "u", 1):
                    pool.wait_ge(s_xn, NORMS.index((0, 1)) + 1)
                    G.memset(cp[:, :, 0:CB], 0.0).then_inc(s_hist, 1)
                pool.wait_ge(s_e, CHOICES.index((layer, n)) + 1)
                with pool.Fori(0, slots // (2 * RING)) as i:
                    for h in range(2):
                        G.tensor_copy(stg[:, h, :], eidx[:, n, bass.ds(i * 2 * RING + h * RING, RING)]).then_inc(s_stg, 1)
                        pool.wait_ge(s_stg, i * 2 + (start // RING + h + 1))
                        for k in range(RING):
                            pool.wait_ge(s_used, i * 2 * RING + (start + h * RING + k + 1))
                            pool.sem_inc(s_turn, 1)
                            G.indirect_dma_start(ring[:, k, :], None, tables[tab],
                                                 bass.IndirectOffsetOnAxis(stg[:, h, k:k + 1], 0)).then_inc(s_g[k], 16)


_INS = ['x_prompt', 'x_sample', 'state_pool', 'state_rnn_conv', 'state_rnn_h', 'state_conv',
        'w_in_even', 'pool_w', 'pool_scale', 'rnn_conv_w', 'rnn_conv_b', 'rg_wa', 'rg_ba', 'rg_wx', 'rg_bx',
        'rg_lambda', 'w_out_even', 'w_glu', 'dw_w', 'dw_b', 'conv_ln_g', 'conv_ln_b', 'w_pw',
        'peer_wq', 'peer_k1', 'peer_k2', 'peer_u', 'peer_v', 'ln_mix_g', 'ln_mix_b', 'ln_ffn_g', 'ln_ffn_b']
_OUTS = [(1, SEQ, D), (DB, DS, D), (1, 1, PB, HALF), (1, 1, RB, HALF), (1, 1, HALF), (1, 1, CB, D),
         (1, DB, PB, HALF), (1, DB, RB, HALF), (1, DB, HALF), (1, DB, CB, D)]


def kernel(**inputs):
    import numpy as _np
    import concourse.bacc as _bacc
    from concourse import mybir as _mybir
    from concourse.bass_utils import run_bass_kernel_spmd as _run

    nc = _bacc.Bacc("TRN2", target_bir_lowering=False, num_devices=1)
    arrays, args = {}, []
    for name in _INS:
        a = _np.ascontiguousarray(inputs[name])
        arrays[f"in_{name}_dram"] = a
        args.append(nc.dram_tensor(f"in_{name}_dram", a.shape, _mybir.dt.from_np(a.dtype), kind="ExternalInput").ap())
    for i, shape in enumerate(_OUTS):
        args.append(nc.dram_tensor(f"out_{i}_dram", shape, _mybir.dt.float32, kind="ExternalOutput").ap())
    build(nc, *args)
    r = _run(nc, [arrays], core_ids=[0])
    return tuple(r.results[0][f"out_{i}_dram"] for i in range(len(_OUTS)))
```

```python
import concourse.bass as bass
from concourse import mybir
from contextlib import ExitStack
import numpy as np

F32 = mybir.dt.float32
I32 = mybir.dt.int32
U32 = mybir.dt.uint32
ALU = mybir.AluOpType
ACT = mybir.ActivationFunctionType
AX = mybir.AxisListType

P = 128
D = 1024
KD = D // P
SEQ, DB, DS = 256, 8, 8
NS = DB * DS
NT = SEQ + NS
HALF = D // 2
JR = HALF // P
PB, RB, CB = 15, 3, 30
CW = 31
HEADS, NK, TOPK = 8, 128, 16
NE = NK * NK
ALPHA = (2.0 * 2) ** 0.25
EPS = 1e-5
RING = 8
ABREAST = 4
A1, B2 = 4, 4
PAIRS = A1 * TOPK + (TOPK - A1) * B2
WSLOT, WC = 4, 256
SMALL_AT = 3
SLOTS = 3
DIAG = 6
V_CW, V_CB, V_BA, V_BX, V_LAM, V_PS, V_DB, V_CG, V_CBT, V_N = 0, 16, 20, 24, 28, 32, 36, 44, 52, 60

TILES = (2, 0, 1)
HEADS_OF = (8, 8, 4)
GANGS = ((2, 0), (1,))
GANG = {n: g for g in GANGS for n in g}
ORD = {n: i for i, n in enumerate(TILES)}
COL = (NS, NS + P, 0)


def width(n):
    return NS if n == 2 else P


NORMS = [(0, 2), (0, 0), (0, 1), (1, 2), (1, 0), (2, 2), (2, 0), (1, 1), (2, 1), (3, 2), (3, 0), (3, 1)]
CHOICES = [(0, 2), (0, 0), (0, 1), (1, 2), (1, 0), (1, 1)]


def span(tiles):
    return sum(width(n) for n in tiles)


def gather_phases():
    out, at = [], 0
    for layer in range(2):
        for tab, n in (("u", 2), ("v", 2), ("u", 0), ("v", 0), ("u", 1), ("v", 1)):
            slots = HEADS_OF[n] * TOPK
            out.append((layer, tab, n, slots, at))
            at += slots
    return out


PHASES = gather_phases()
ROWS = PHASES[-1][4] + PHASES[-1][3]


def psum_groups():
    g = []

    def x_turned(layer, part, tiles):
        return [("xT", layer, part, n, q) for n in tiles for q in range(2)]

    def front(layer, tiles):
        return (x_turned(layer, 1, tiles) + [("q", layer, tiles, c) for c in range(HEADS)]
                + [("s", layer, n, i) for n in tiles for i in range(HEADS_OF[n] // 2)])

    for gang in GANGS:
        g += x_turned(0, 0, gang)
        for ft in range(12):
            g += [("z0", gang, ft)]
            if gang == GANGS[0] and ft == SMALL_AT:
                g += [("vec",), ("dw", 0), ("dw", 1), ("key",), ("stp",), ("srh",)]
        for n in gang:
            g += [("st0", n, k) for k in range(2) if n]
            g += [("ya", n, j) for j in range(JR)] + [(w, n, j) for j in range(JR) for w in ("ga", "gx")]
            g += [("h0", n)] if n else []
            g += [("o", 0, n, blk) for blk in range(D // WC)] + front(0, (n,))
    g += [("fold", 0, h) for h in range(2)]
    for gang in GANGS:
        g += x_turned(1, 0, gang) + [("scv", p, q) for p in range(2) for q in range(2) if 2 in gang]
        g += [("z1", gang, f) for f in range(KD)]
        g += [("cst", gang[0], k) for k in range(4 if 2 in gang else 2)]
        g += [("cv", n, f) for f in range(KD) for n in gang] + [(w, n) for n in gang for w in ("mu", "var")]
        g += [("o", 1, n, blk) for blk in range(D // WC) for n in gang]
        g += front(1, gang)
    g += [("fold", 1, h) for h in range(2)]
    return g


GROUPS = psum_groups()
GID = {name: i for i, name in enumerate(GROUPS)}


def weight_blocks():
    out = []

    def queries(layer, tiles):
        return [("q", layer, c, ("q", layer, tiles, c)) for c in range(HEADS)]

    for gang in GANGS:
        out += [("in", 0, c, ("z0", gang, 2 * c + 1)) for c in range(6)]
        for n in gang:
            out += [("out", 0, c, ("o", 0, n, c)) for c in range(4)] + queries(0, (n,))
    for gang in GANGS:
        out += [("glu", 0, c, ("z1", gang, c)) for c in range(KD)]
        out += [("pw", 0, c, ("o", 1, gang[-1], c)) for c in range(4)]
        out += queries(1, gang)
    return out


BLOCKS = weight_blocks()


def build(nc, x_prompt, x_sample, state_pool, state_rnn_conv, state_rnn_h, state_conv,
          w_in_even, pool_w, pool_scale, rnn_conv_w, rnn_conv_b, rg_wa, rg_ba, rg_wx, rg_bx,
          rg_lambda, w_out_even, w_glu, dw_w, dw_b, conv_ln_g, conv_ln_b, w_pw,
          peer_wq, peer_k1, peer_k2, peer_u, peer_v, ln_mix_g, ln_mix_b, ln_ffn_g, ln_ffn_b,
          y_prompt, y_sample, o_pool_p, o_rconv_p, o_h_p, o_conv_p, o_pool_s, o_rconv_s, o_h_s, o_conv_s):
    ctx = ExitStack()
    with ctx:
        def sb(name, shape, dt=F32, stack=ctx):
            return stack.enter_context(nc.sbuf_tensor(name, shape, dt))

        def sem(name):
            return ctx.enter_context(nc.semaphore(name))

        ident = sb("ident", [P, P])
        foldm = sb("foldm", [P, P])
        mean_m = sb("mean_m", [P, P])
        iota_i = sb("iota_i", [P, 16], I32)
        iota_f = sb("iota_f", [P, 16])
        inv_cnt = sb("inv_cnt", [P, JR, 16])
        vecs = sb("vecs", [P, V_N])
        taps = sb("taps", [P, CW * KD])
        spc = sb("spc", [P, JR])
        keyT = sb("keyT", [P, 4, P])
        poolw = sb("poolw", [P, JR, P])
        bda = sb("bda", [P, JR, P])
        bdx = sb("bdx", [P, JR, P])
        sm = sb("sm", [P, 24])
        x = sb("x", [P, 3, D])
        xT = sb("xT", [P, KD, NT])
        yT = [sb("yT_s", [P, KD, 2, NS]), sb("yT_p", [P, KD, 1, SEQ])]
        lnp = sb("lnp", [P, 2, 2, D])
        wr = sb("wr", [P, WSLOT, KD, WC])
        hlast_s = sb("hlast_s", [P, JR, DB])
        hlast_p = sb("hlast_p", [P, JR])
        bn = sb("bn", [P, 2, 6])
        mv = sb("mv", [P, 3, 8])
        so = sb("so", [P, SLOTS, HALF])
        qT_p = sb("qT", [P, 16, P])
        qT_s = so[:, 0:2, :].rearrange("p a (f t) -> p (a f) t", t=P)
        qT = [qT_p[:], qT_p[:], qT_s]
        sc = sb("sc", [P, 16, NK])
        tv = sb("tv", [P, 16, TOPK])
        ti = sb("ti", [P, 16, TOPK], U32)
        tif = sb("tif", [P, 16, TOPK])
        spare = sb("spare", [P, ABREAST, NK])
        oh = sb("oh", [P, HEADS, TOPK, TOPK])
        cand = oh[:].rearrange("p h a b -> p (h a b)")[:, 0:HEADS * PAIRS].rearrange("p (h c) -> p h c", h=HEADS)
        sv = sb("sv", [P, HEADS, TOPK])
        ci = sb("ci", [P, HEADS, TOPK], U32)
        cab = sb("cab", [P, 2, HEADS, TOPK], U32)
        cabf = sb("cabf", [P, 2, HEADS, TOPK])
        beyond = sb("beyond", [P, HEADS, TOPK])
        key_no = sb("key_no", [P, 2, HEADS, TOPK])
        eidx = sb("eidx", [P, 3, NK], I32)
        gate = sb("gate", [P, 3, HEADS, TOPK])
        gsm = sb("gsm", [P, HEADS])
        actv = sb("actv", [P, 3, NK])
        acg = sb("acg", [P, NK])
        stg = sb("stg", [P, 2, RING], I32)
        ring = sb("ring", [P, RING, D])
        acc = sb("acc", [P, 2, D])
        facc = sb("facc", [P, D])
        rows_v, rows_dw, rows_key = ring[0:V_N, 0, 0:P], ring[0:124, 0, 128:384], ring[:, 1, 0:512]
        rows_sp, rows_sr, rows_sh = ring[0:DB * PB, 2, 0:HALF], ring[0:DB * RB, 3, 0:HALF], ring[0:DB, 4, 0:HALF]

        m0 = ExitStack()
        pp = sb("pp", [P, JR, PB + SEQ], stack=m0)
        ps_ = sb("ps", [P, JR, DB, PB + DS], stack=m0)
        rp = sb("rp", [P, JR, RB + SEQ], stack=m0)
        rs = sb("rs", [P, JR, DB, RB + DS], stack=m0)
        dps = sb("dps", [P, JR, DB * PB], stack=m0)
        drs = sb("drs", [P, JR, DB * RB], stack=m0)
        h0 = sb("h0", [P, JR, DB], stack=m0)
        wab = sb("wab", [P, 2, JR, DB * (PB + DS)], stack=m0)
        rnn = sb("rnn", [P, 2, JR, P], stack=m0)
        m0.close()
        rnn_p = [qT_p[:, JR * i:JR * (i + 1), :] for i in range(4)] + [rnn[:, i] for i in range(2)]
        rnn_s = [t.rearrange("p j t -> p (j t)")[:, 0:JR * NS].rearrange("p (j t) -> p j t", j=JR) for t in rnn_p]
        m1 = ExitStack()
        cp = sb("cp", [P, KD, CB + SEQ], stack=m1)
        cs = sb("cs", [P, KD, DB, CB + DS], stack=m1)
        sg = sb("sg", [P, 2, NS + P], stack=m1)
        sq = oh[:].rearrange("p h a b -> p (h a b)")
        mub = sb("mub", [P, P], stack=m1)
        rsb = sb("rsb", [P, 3, P], stack=m1)
        diag = sb("diag", [P, DIAG, P], stack=m1)
        m1.close()
        rows_sc = sq[0:120, 0:2 * D].rearrange("p (h c) -> p h c", h=2)
        dcs = sq[:, 0:KD * DB * CB].rearrange("p (f r) -> p f r", f=KD)

        pb = [ctx.enter_context(nc.psum_tensor(f"bank{b}", [P, 512], F32)) for b in range(8)]

        s_mm = sem("s_mm")
        s_moved = [sem(f"s_moved{b}") for b in range(8)]
        s_x = [sem(f"s_x{n}") for n in range(3)]
        s_vec = sem("s_vec")
        s_key = sem("s_key")
        s_st = sem("s_st")
        s_bd = sem("s_bd")
        s_scv = sem("s_scv")
        s_w = [sem(f"s_w{i}") for i in range(WSLOT)]
        s_ln = [sem(f"s_ln{i}") for i in range(2)]
        s_so = [sem(f"s_so{i}") for i in range(SLOTS)]
        s_out = sem("s_out")
        s_cst = sem("s_cst")
        s_bz = sem("s_bz")
        s_hist = sem("s_hist")
        s_dv = sem("s_dv")
        s_lam1 = sem("s_lam1")
        s_lam2 = sem("s_lam2")
        s_spc = sem("s_spc")
        s_rows = sem("s_rows")
        s_pooled = sem("s_pooled")
        s_xc = sem("s_xc")
        s_th = sem("s_th")
        s_q2 = sem("s_q2")
        s_rt = sem("s_rt")
        s_yb = sem("s_yb")
        s_var = sem("s_var")
        s_sd = sem("s_sd")
        s_xn = sem("s_xn")
        s_sub = sem("s_sub")
        s_ex = sem("s_ex")
        s_sel = sem("s_sel")
        s_e = sem("s_e")
        s_g = [sem(f"s_g{i}") for i in range(RING)]
        s_used = sem("s_used")
        s_turn = sem("s_turn")
        s_stg = sem("s_stg")
        s_act = sem("s_act")
        s_gel = sem("s_gel")
        s_facc = sem("s_facc")
        s_sig = sem("s_sig")
        s_glu = sem("s_glu")
        s_diag = sem("s_diag")
        s_cvf = sem("s_cvf")
        s_cm = sem("s_cm")
        s_csq = sem("s_csq")
        s_cve = sem("s_cve")
        s_csd = sem("s_csd")
        s_cn = sem("s_cn")
        s_silu = sem("s_silu")

        def x_cols(n):
            return xT[:, :, COL[n]:COL[n] + width(n)]

        def x_of(tiles):
            return xT[:, :, COL[tiles[0]]:COL[tiles[-1]] + width(tiles[-1])]

        def y_cols(n):
            return yT[0][:] if n == 2 else yT[1][:, :, :, n * P:(n + 1) * P]

        def in_sequences(n, t):
            return t.rearrange("p (b s) -> p b s", b=DB) if n == 2 else t

        def extended(n, sample, prompt, past):
            if n == 2:
                return lambda j: sample[:, j]
            return lambda j: prompt[:, j, n * P:past + (n + 1) * P]

        pool_x = [extended(n, ps_, pp, PB) for n in range(3)]
        conv_x = [extended(n, rs, rp, RB) for n in range(3)]
        glu_x = [extended(n, cs, cp, CB) for n in range(3)]
        gates_x = [rnn_p, rnn_p, rnn_s]

        def moved(eng, name):
            g = GID[name]
            eng.wait_ge(s_moved[g % 8], g // 8 + 1)

        def filled(eng, name):
            eng.wait_ge(s_mm, GID[name] + 1)
            return pb[GID[name] % 8], s_moved[GID[name] % 8]

        block = ctx.enter_context(nc.Block())

        @block.sync
        def _(sp):
            def rows_of_weights(name):
                return {"in": w_in_even[0], "out": w_out_even[0], "pw": w_pw[0]}[name]

            def weights(n0, n1):
                for i in range(n0, n1):
                    name, layer, c, _ = BLOCKS[i]
                    if i >= WSLOT:
                        sp.wait_ge(s_mm, GID[BLOCKS[i - WSLOT][3]] + 1)
                    slot = i % WSLOT
                    if name == "glu":
                        v = w_glu[0].rearrange("(k p) (a n) -> p a k n", p=P, a=2)
                        for a in range(2):
                            sp.dma_start(wr[:, slot, :, a * P:(a + 1) * P], v[:, a, :, c * P:(c + 1) * P]).then_inc(s_w[slot], 16)
                    else:
                        w = peer_wq[layer] if name == "q" else rows_of_weights(name)
                        sp.dma_start(wr[:, slot], w.rearrange("(k p) n -> p k n", p=P)[:, :, c * WC:(c + 1) * WC])\
                          .then_inc(s_w[slot], 16)

            for h in range(2):
                sp.dma_start(x[h * NS:(h + 1) * NS, 2, :], x_sample.rearrange("b s d -> (b s) d")).then_inc(s_x[2], 16)
            sp.dma_start(x[:, 0, :], x_prompt[0, 0:P, :]).then_inc(s_x[0], 16)
            weights(0, 2)
            for src, r0, r1 in ((rnn_conv_w[0].rearrange("w (j p) -> (w j) p", p=P), V_CW, V_CB),
                                (rnn_conv_b.rearrange("a (j p) -> (a j) p", p=P), V_CB, V_BA),
                                (rg_ba.rearrange("a (j p) -> (a j) p", p=P), V_BA, V_BX),
                                (rg_bx.rearrange("a (j p) -> (a j) p", p=P), V_BX, V_LAM),
                                (rg_lambda.rearrange("a (j p) -> (a j) p", p=P), V_LAM, V_PS),
                                (pool_scale.rearrange("a (j p) -> (a j) p", p=P), V_PS, V_DB),
                                (dw_b.rearrange("a (j p) -> (a j) p", p=P), V_DB, V_CG),
                                (conv_ln_g.rearrange("a (j p) -> (a j) p", p=P), V_CG, V_CBT),
                                (conv_ln_b.rearrange("a (j p) -> (a j) p", p=P), V_CBT, V_N)):
                sp.dma_start(rows_v[r0:r1, :], src).then_inc(s_vec, 16)
            dwr = dw_w[0].rearrange("w (f p) -> (w f) p", p=P)
            for h in range(2):
                sp.dma_start(rows_dw[:, h * P:(h + 1) * P], dwr[h * 124:(h + 1) * 124, :]).then_inc(s_vec, 16)
            for layer in range(2):
                for i, k in enumerate((peer_k1, peer_k2)):
                    sp.dma_start(rows_key[:, (2 * layer + i) * P:(2 * layer + i + 1) * P], k[layer]).then_inc(s_key, 16)
            sp.dma_start(rows_sp, state_pool[0].rearrange("b t c -> (b t) c")).then_inc(s_st, 16)
            sp.dma_start(rows_sr, state_rnn_conv[0].rearrange("b t c -> (b t) c")).then_inc(s_st, 16)
            sp.dma_start(rows_sh, state_rnn_h[0]).then_inc(s_st, 16)
            weights(2, WSLOT)
            sp.dma_start(poolw[:], pool_w[0].rearrange("g c d -> c g d")).then_inc(s_bd, 16)
            sp.wait_ge(s_bz, 2)
            for dst, src in ((bda, rg_wa), (bdx, rg_wx)):
                v = src[0].rearrange("(j h) i o -> h i j o", h=2)
                for h in range(2):
                    sp.dma_start(dst[64 * h:64 * h + 64, :, 64 * h:64 * h + 64], v[h]).then_inc(s_bd, 16)
            sp.dma_start(x[:, 1, :], x_prompt[0, P:2 * P, :]).then_inc(s_x[1], 16)

            def ln_rows(i):
                layer = i // 2
                for j, v in enumerate((ln_ffn_g, ln_ffn_b) if i % 2 else (ln_mix_g, ln_mix_b)):
                    sp.dma_start(lnp[:, i % 2, j, :], v[layer:layer + 1, :].to_broadcast([P, D])).then_inc(s_ln[i % 2], 16)

            ln_rows(0)
            ln_rows(1)
            layer1 = [b[0] for b in BLOCKS].index("glu")
            gang1 = [b[3] for b in BLOCKS].index(("z1", GANGS[1], 0))
            weights(WSLOT, layer1)
            sp.wait_ge(s_xn, NORMS.index((0, 1)) + 1)
            ln_rows(2)
            sp.wait_ge(s_e, CHOICES.index((0, 1)) + 1)
            scr_ = state_conv[0].rearrange("b t c -> (b t) c")
            for p in range(2):
                sp.dma_start(rows_sc[:, p, :], scr_[120 * p:120 * p + 120, :]).then_inc(s_scv, 16)
            weights(layer1, gang1)
            sp.wait_ge(s_xn, NORMS.index((1, 1)) + 1)
            ln_rows(3)
            weights(gang1, len(BLOCKS))
            sp.wait_ge(s_xn, NORMS.index((3, 2)) + 1)
            sp.dma_start(y_sample.rearrange("b s d -> (b s) d"), x[0:NS, 2, :]).then_inc(s_out, 16)
            for n in range(2):
                sp.wait_ge(s_xn, NORMS.index((3, n)) + 1)
                sp.dma_start(y_prompt[0, n * P:(n + 1) * P, :], x[:, n, :]).then_inc(s_out, 16)
            sp.wait_ge(s_out, 48)
            for i in range(SLOTS):
                sp.wait_ge(s_so[i], 16 * 4)

        @block.tensor
        def _(pe):
            todo = list(GROUPS)
            block_no = [0]
            landed = [0] * WSLOT

            def begin(name):
                assert todo.pop(0) == name, name
                g = GID[name]
                if g >= 8:
                    pe.wait_ge(s_moved[g % 8], g // 8)
                return pb[g % 8]

            def next_block(name):
                i = block_no[0]
                block_no[0] += 1
                assert BLOCKS[i][0] == name
                landed[i % WSLOT] += 32 if name == "glu" else 16
                pe.wait_ge(s_w[i % WSLOT], landed[i % WSLOT])
                return wr[:, i % WSLOT]

            def project(out, w, rhs):
                for k in range(KD):
                    last = nc.tensor.matmul(out, w[:, k, :], rhs[:, k, :], start=(k == 0), stop=(k == KD - 1))
                return last

            def x_transposes(layer, part, tiles):
                for n in tiles:
                    if layer or part:
                        pe.wait_ge(s_xn, NORMS.index((2 * layer + part - 1, n)) + 1)
                    else:
                        pe.wait_ge(s_x[n], 32 if n == 2 else 16)
                    rows = width(n)
                    for q in range(2):
                        b = begin(("xT", layer, part, n, q))
                        for i in range(4):
                            f = 4 * q + i
                            last = nc.tensor.transpose(b[:, i * rows:(i + 1) * rows],
                                                       x[0:rows, n, f * P:(f + 1) * P], ident[0:rows, 0:rows])
                        last.then_inc(s_mm, 1)

            def project_out(layer, tiles):
                for blk in range(D // WC):
                    w = next_block("pw" if layer else "out")
                    for n in tiles:
                        y = y_cols(n).rearrange("p k a t -> p k (a t)")
                        b = begin(("o", layer, n, blk))
                        for k in range(KD):
                            last = nc.tensor.matmul(b[:, 0:WC], y[:, k, :], w[:, k, :], start=(k == 0), stop=(k == KD - 1))
                        last.then_inc(s_mm, 1)

            def front(layer, tiles):
                x_transposes(layer, 1, tiles)
                moved(pe, ("xT", layer, 1, tiles[-1], 1))
                for c in range(HEADS):
                    w = next_block("q")
                    b = begin(("q", layer, tiles, c))
                    w_ = span(tiles)
                    for i in range(2):
                        if w_ < P:
                            for k in range(KD):
                                last = nc.tensor.matmul(b[:, i * P:(i + 1) * P].rearrange("p (a t) -> p a t", t=w_),
                                                        w[:, k, i * P:(i + 1) * P],
                                                        x_of(tiles)[:, k, :].unsqueeze(1).to_broadcast([P, P // w_, w_]),
                                                        start=(k == 0), stop=(k == KD - 1))
                        else:
                            last = project(b[:, i * w_:(i + 1) * w_], w[:, :, i * P:(i + 1) * P], x_of(tiles))
                    last.then_inc(s_mm, 1)
                for n in tiles:
                    moved(pe, ("q", layer, tiles, HEADS - 1))
                    for i in range(HEADS_OF[n] // 2):
                        b = begin(("s", layer, n, i))
                        for j in range(4):
                            f = 4 * i + j
                            last = nc.tensor.matmul(b[:, j * P:(j + 1) * P], qT[n][:, f, :], keyT[:, 2 * layer + f % 2, :],
                                                    start=True, stop=True)
                        last.then_inc(s_mm, 1)

            def fold(layer):
                pe.wait_ge(s_cst, 7)
                pe.wait_ge(s_facc, layer + 1)
                for h in range(2):
                    b = begin(("fold", layer, h))
                    nc.tensor.matmul(b[:, :], foldm[:], facc[:, h * 512:(h + 1) * 512],
                                     start=True, stop=True).then_inc(s_mm, 1)

            def turn_states(name, srcs, rows):
                b = begin(name)
                for i, src in enumerate(srcs):
                    last = nc.tensor.transpose(b[0:rows, i * P:(i + 1) * P], src, ident[:])
                last.then_inc(s_mm, 1)

            def small_inputs():
                pe.wait_ge(s_vec, 11 * 16)
                b = begin(("vec",))
                nc.tensor.transpose(b[:, 0:V_N], rows_v, ident[0:V_N, 0:V_N]).then_inc(s_mm, 1)
                for h in range(2):
                    b = begin(("dw", h))
                    nc.tensor.transpose(b[:, 0:124], rows_dw[:, h * P:(h + 1) * P], ident[0:124, 0:124]).then_inc(s_mm, 1)
                pe.wait_ge(s_key, 64)
                b = begin(("key",))
                for i in range(4):
                    last = nc.tensor.transpose(b[:, i * P:(i + 1) * P], rows_key[:, i * P:(i + 1) * P], ident[:])
                last.then_inc(s_mm, 1)
                pe.wait_ge(s_st, 48)
                b = begin(("stp",))
                for j in range(JR):
                    last = nc.tensor.transpose(b[:, j * 120:(j + 1) * 120], rows_sp[:, j * P:(j + 1) * P], ident[0:120, 0:120])
                last.then_inc(s_mm, 1)
                b = begin(("srh",))
                for j in range(JR):
                    nc.tensor.transpose(b[:, j * 24:(j + 1) * 24], rows_sr[:, j * P:(j + 1) * P], ident[0:24, 0:24])
                for j in range(JR):
                    last = nc.tensor.transpose(b[:, 96 + j * 8:104 + j * 8], rows_sh[:, j * P:(j + 1) * P], ident[0:8, 0:8])
                last.then_inc(s_mm, 1)

            def even_in(gang):
                x_transposes(0, 0, gang)
                moved(pe, ("xT", 0, 0, gang[-1], 1))
                cols = span(gang)
                for c in range(6):
                    w = next_block("in")
                    for i in range(2):
                        b = begin(("z0", gang, 2 * c + i))
                        project(b[:, 0:cols], w[:, :, i * P:(i + 1) * P], x_of(gang)).then_inc(s_mm, 1)
                        if gang == GANGS[0] and 2 * c + i == SMALL_AT:
                            small_inputs()

            def even_mixer(n):
                cols = width(n)
                if n == 2:
                    pe.wait_ge(s_rows, 2)
                    for k, (buf, rows) in enumerate(((dps, DB * PB), (drs, DB * RB))):
                        turn_states(("st0", n, k), [buf[:, j, :] for j in range(JR)], rows)
                elif n == 1:
                    moved(pe, ("z0", GANG[n], 7))
                    for k, (buf, rows) in enumerate(((pp, PB), (rp, RB))):
                        turn_states(("st0", n, k), [buf[:, j, SEQ:] for j in range(JR)], rows)
                pe.wait_ge(s_bd, 16 * 5)
                for j in range(JR):
                    pe.wait_ge(s_pooled, ORD[n] * JR + j + 1)
                    b = begin(("ya", n, j))
                    nc.tensor.matmul(b[:, 0:cols], poolw[:, j, :], y_cols(n)[:, j, 0, :], start=True, stop=True).then_inc(s_mm, 1)
                for j in range(JR):
                    pe.wait_ge(s_xc, ORD[n] * JR + j + 1)
                    for w, m in (("ga", bda), ("gx", bdx)):
                        b = begin((w, n, j))
                        nc.tensor.matmul(b[:, 0:cols], m[:, j, :], gates_x[n][0][:, j, :], start=True, stop=True).then_inc(s_mm, 1)
                pe.wait_ge(s_yb, ORD[n] + 1)
                if n == 2:
                    turn_states(("h0", n), [hlast_s[:, j, :] for j in range(JR)], DB)
                elif n == 1:
                    turn_states(("h0", n), [hlast_p[:, j:j + 1] for j in range(JR)], 1)
                moved(pe, ("ya", n, JR - 1))
                project_out(0, (n,))

            def odd_mixer(gang):
                x_transposes(1, 0, gang)
                if 2 in gang:
                    pe.wait_ge(s_scv, 32)
                    for p in range(2):
                        for q in range(2):
                            b = begin(("scv", p, q))
                            for i in range(4):
                                f = 4 * q + i
                                last = nc.tensor.transpose(b[:, i * 120:(i + 1) * 120], rows_sc[:, p, f * P:(f + 1) * P],
                                                           ident[0:120, 0:120])
                            last.then_inc(s_mm, 1)
                moved(pe, ("xT", 1, 0, gang[-1], 1))
                for f in range(KD):
                    w = next_block("glu")
                    b = begin(("z1", gang, f))
                    project(b[:, 0:span(gang)], w[:, :, 0:P], x_of(gang))
                    project(b[:, 256:256 + span(gang)], w[:, :, P:2 * P], x_of(gang)).then_inc(s_mm, 1)
                if 2 in gang:
                    pe.wait_ge(s_rows, 3)
                    for k in range(4):
                        p, q = k // 2, k % 2
                        turn_states(("cst", 2, k), [dcs[:, 4 * q + i, 120 * p:120 * p + 120] for i in range(4)], 120)
                else:
                    pe.wait_ge(s_glu, 2 * KD)
                    for k in range(2):
                        turn_states(("cst", 1, k), [cp[:, 4 * k + i, SEQ:] for i in range(4)], CB)
                pe.wait_ge(s_glu, KD * (GANGS.index(gang) + 1))
                d = KD * CW * GANGS.index(gang)
                for f in range(KD):
                    banks = {n: begin(("cv", n, f)) for n in gang}
                    for w in range(CW):
                        pe.wait_ge(s_diag, d + 1)
                        for n in gang:
                            src = glu_x[n](f)[..., w:w + (DS if n == 2 else P)]
                            last = nc.tensor.matmul(in_sequences(n, banks[n][:, 0:width(n)]), diag[:, d % DIAG, :], src,
                                                    start=(w == 0), stop=(w == CW - 1))
                            if w == CW - 1:
                                last.then_inc(s_mm, 1)
                        if w < CW - 1:
                            last.then_inc(s_cvf, 1)
                        d += 1
                for n in gang:
                    cols = width(n)
                    moved(pe, ("cv", n, KD - 1))
                    b = begin(("mu", n))
                    for f in range(KD):
                        last = nc.tensor.matmul(b[:, 0:cols], mean_m[:], y_cols(n)[:, f, 0, :], start=(f == 0), stop=(f == KD - 1))
                    last.then_inc(s_mm, 1)
                    pe.wait_ge(s_csq, ORD[n] + 1)
                    b = begin(("var", n))
                    for f in range(KD):
                        last = nc.tensor.matmul(b[:, 0:cols], mean_m[:], sq[:, f * cols:(f + 1) * cols],
                                                start=(f == 0), stop=(f == KD - 1))
                    last.then_inc(s_mm, 1)
                pe.wait_ge(s_silu, KD * (ORD[gang[-1]] + 1))
                project_out(1, gang)

            pe.wait_ge(s_cst, 5)
            for gang in GANGS:
                even_in(gang)
                for n in gang:
                    even_mixer(n)
                    front(0, (n,))
            fold(0)
            for gang in GANGS:
                odd_mixer(gang)
                front(1, gang)
            fold(1)
            assert not todo and block_no[0] == len(BLOCKS)

        @block.scalar
        def _(act):
            A = nc.scalar.activation
            n_out = [0]
            n_diag = [0]

            def store_rows(name, rows, dst):
                k = n_out[0]
                n_out[0] += 1
                if k >= SLOTS:
                    act.wait_ge(s_so[k % SLOTS], 16 * (k // SLOTS))
                b, free = filled(act, name)
                A(so[0:rows, k % SLOTS, :], b[0:rows, :], ACT.Copy).then_inc(free, 1)
                moved(act, name)
                act.dma_start(dst, so[0:rows, k % SLOTS, :]).then_inc(s_so[k % SLOTS], 16)

            def x_columns(layer, part, tiles):
                for n in tiles:
                    for q in range(2):
                        b, free = filled(act, ("xT", layer, part, n, q))
                        A(x_cols(n)[:, 4 * q:4 * q + 4, :],
                          b[:, 0:4 * width(n)].rearrange("p (f t) -> p f t", f=4), ACT.Copy).then_inc(free, 1)

            def root(i, n):
                act.wait_ge(s_var, NORMS.index((i, n)) + 1)
                A(mv[:, n, 3:4], mv[:, n, 2:3], ACT.Sqrt).then_inc(s_sd, 1)

            def queries(layer, tiles):
                x_columns(layer, 1, tiles)
                if 2 in tiles:
                    for i in range(SLOTS):
                        act.wait_ge(s_so[i], 16 * ((n_out[0] - i + SLOTS - 1) // SLOTS))
                for c in range(HEADS):
                    b, free = filled(act, ("q", layer, tiles, c))
                    both = b[:, 0:2 * max(P, span(tiles))].rearrange("p (f t) -> p f t", f=2)
                    for n in tiles:
                        at = COL[n] - COL[tiles[0]]
                        if n < 2:
                            dst = qT[n][:, 2 * c:2 * c + 2, :]
                        else:
                            dst = qT[n][:, 2 * (c % 4):2 * (c % 4) + 2, (c // 4) * NS:(c // 4 + 1) * NS]
                        last = A(dst, both[:, :, at:at + width(n)], ACT.Copy)
                    last.then_inc(free, 1)

            def scores(layer, n):
                c0 = CHOICES.index((layer, n))
                if c0:
                    act.wait_ge(s_sel, c0)
                for i in range(HEADS_OF[n] // 2):
                    b, free = filled(act, ("s", layer, n, i))
                    A(sc[:, 4 * i:4 * i + 4, :].rearrange("p a k -> p (a k)"), b[:], ACT.Copy).then_inc(free, 1)

            def front(layer, n):
                queries(layer, (n,))
                scores(layer, n)

            def exps(layer, n):
                heads = HEADS_OF[n]
                act.wait_ge(s_sub, CHOICES.index((layer, n)) + 1)
                A(gate[:, n, 0:heads, :], gate[:, n, 0:heads, :], ACT.Exp).then_inc(s_ex, 1)

            def gelus(layer, n):
                k = [(l, m) for l, t, m, _, _ in PHASES if t == "u"].index((layer, n))
                act.wait_ge(s_act, k + 1)
                slots = HEADS_OF[n] * TOPK
                A(acg[:, 0:slots], actv[:, n, 0:slots], ACT.Gelu_apprx_tanh).then_inc(s_gel, 1)

            def small_inputs():
                b, free = filled(act, ("vec",))
                A(vecs[:], b[:, 0:V_N], ACT.Copy).then_inc(free, 1)
                for h in range(2):
                    b, free = filled(act, ("dw", h))
                    A(taps[:, h * 124:(h + 1) * 124], b[:, 0:124], ACT.Copy).then_inc(free, 1)
                b, free = filled(act, ("key",))
                A(keyT[:].rearrange("p a k -> p (a k)"), b[:], ACT.Copy).then_inc(free, 1)
                b, free = filled(act, ("stp",))
                A(ps_[:, :, :, 0:PB], b[:, 0:480].rearrange("p (j b t) -> p j b t", j=JR, b=DB), ACT.Copy).then_inc(free, 1)
                b, free = filled(act, ("srh",))
                A(rs[:, :, :, 0:RB], b[:, 0:96].rearrange("p (j b t) -> p j b t", j=JR, b=DB), ACT.Copy)
                A(h0[:], b[:, 96:128].rearrange("p (j b) -> p j b", j=JR), ACT.Copy).then_inc(free, 1)
                act.wait_ge(s_lam1, 1)
                A(sm[:, 4:8], sm[:, 0:4], ACT.Exp).then_inc(s_lam2, 1)

            def even_in(gang):
                x_columns(0, 0, gang)
                for ft in range(12):
                    b, free = filled(act, ("z0", gang, ft))
                    for n in gang:
                        at = COL[n] - COL[gang[0]]
                        src = b[:, at:at + width(n)]
                        if ft < 8:
                            dst = (pool_x, conv_x)[ft // 4][n](ft % 4)[..., (PB, RB)[ft // 4]:]
                            last = A(dst, in_sequences(n, src), ACT.Copy)
                        else:
                            last = A(y_cols(n)[:, JR + ft - 8, 0, :], src, ACT.Gelu_apprx_tanh)
                    last.then_inc(free, 1)
                    if gang == GANGS[0] and ft == SMALL_AT:
                        small_inputs()

            def even_mixer(n):
                cols = width(n)
                if n == 2:
                    moved(act, ("z0", GANG[n], 7))
                    for dst, src in ((dps, ps_), (drs, rs)):
                        for j in range(JR):
                            last = A(dst[:, j, :].rearrange("p (b t) -> p b t", b=DB), src[:, j, :, DS:], ACT.Copy)
                        last.then_inc(s_rows, 1)
                if n:
                    outs = ((o_pool_s, DB * PB), (o_rconv_s, DB * RB)) if n == 2 else ((o_pool_p, PB), (o_rconv_p, RB))
                    for k, (dst, rows) in enumerate(outs):
                        store_rows(("st0", n, k), rows, dst[0].rearrange("b t c -> (b t) c"))
                for j in range(JR):
                    b, free = filled(act, ("ya", n, j))
                    copies = 2 if n == 2 else 1
                    A(y_cols(n)[:, j], b[:, 0:cols].unsqueeze(1).to_broadcast([P, copies, cols]), ACT.Identity,
                      scale=vecs[:, V_PS + j:V_PS + j + 1]).then_inc(free, 1)
                buf = gates_x[n]
                for j in range(JR):
                    for w, i, v in (("ga", 1, V_BA), ("gx", 2, V_BX)):
                        b, free = filled(act, (w, n, j))
                        A(buf[i][:, j, :], b[:, 0:cols], ACT.Sigmoid, bias=vecs[:, v + j:v + j + 1]).then_inc(free, 1)
                act.wait_ge(s_spc, 1)
                moved(act, ("gx", n, JR - 1))
                for j in range(JR):
                    A(buf[3][:, j, :], buf[1][:, j, :], ACT.Tanh, scale=spc[:, j:j + 1]).then_inc(s_th, 1)
                act.wait_ge(s_q2, ORD[n] + 1)
                A(buf[3], buf[1], ACT.Sqrt).then_inc(s_rt, 1)
                if n:
                    store_rows(("h0", n), DB if n == 2 else 1, (o_h_s if n == 2 else o_h_p)[0])

            def odd_mixer(gang, meanwhile):
                x_columns(1, 0, gang)
                if 2 in gang:
                    for p in range(2):
                        for q in range(2):
                            b, free = filled(act, ("scv", p, q))
                            for i in range(4):
                                last = A(cs[:, 4 * q + i, 4 * p:4 * p + 4, 0:CB],
                                         b[:, 120 * i:120 * i + 120].rearrange("p (b t) -> p b t", b=4), ACT.Copy)
                            last.then_inc(free, 1)
                k = KD * GANGS.index(gang)
                for f in range(KD):
                    b, _ = filled(act, ("z1", gang, f))
                    if k >= 2:
                        act.wait_ge(s_glu, k - 1)
                    A(sg[:, k % 2, 0:span(gang)], b[:, 256:256 + span(gang)], ACT.Sigmoid).then_inc(s_sig, 1)
                    k += 1
                    meanwhile.get(("glu", f), nothing)()
                if 2 in gang:
                    act.wait_ge(s_glu, k)
                    moved(act, ("scv", 1, 1))
                    for f in range(KD):
                        last = A(dcs[:, f, :].rearrange("p (b t) -> p b t", b=DB), cs[:, f, :, DS:], ACT.Copy)
                    last.then_inc(s_rows, 1)
                    outs = [(120, o_conv_s[0].rearrange("b t c -> (b t) c")[120 * p:120 * p + 120, q * HALF:(q + 1) * HALF])
                            for p in range(2) for q in range(2)]
                else:
                    outs = [(CB, o_conv_p[0, 0, :, q * HALF:(q + 1) * HALF]) for q in range(2)]
                for i, (rows, dst) in enumerate(outs):
                    store_rows(("cst", gang[0], i), rows, dst)
                for f in range(KD):
                    meanwhile.get(("conv", f), nothing)()
                    for w in range(CW):
                        d = n_diag[0]
                        n_diag[0] += 1
                        if d >= DIAG:
                            g, t = divmod(d - DIAG, CW)
                            if t == CW - 1:
                                act.wait_ge(s_mm, GID[("cv", GANGS[g // KD][-1], g % KD)] + 1)
                            else:
                                act.wait_ge(s_cvf, (d - DIAG) - g + 1)
                        A(diag[:, d % DIAG, :], ident[:], ACT.Copy, scale=taps[:, w * KD + f:w * KD + f + 1]).then_inc(s_diag, 1)
                    if f:
                        conv_out(gang, f - 1)
                conv_out(gang, KD - 1)

            def nothing():
                pass

            def conv_norm(n):
                cols = width(n)
                b, free = filled(act, ("mu", n))
                A(mub[:, 0:cols], b[:, 0:cols], ACT.Copy).then_inc(free, 1)
                act.wait_ge(s_cm, ORD[n] + 1)
                squares = sq[:, 0:KD * cols].rearrange("p (f t) -> p f t", f=KD)
                A(squares, y_cols(n)[:, :, 0, :], ACT.Square).then_inc(s_csq, 1)
                act.wait_ge(s_cve, ORD[n] + 1)
                A(rsb[:, 1, 0:cols], rsb[:, 0, 0:cols], ACT.Sqrt).then_inc(s_csd, 1)
                act.wait_ge(s_cn, ORD[n] + 1)
                for f in range(KD):
                    copies = 2 if n == 2 else 1
                    A(y_cols(n)[:, f], squares[:, f, :].unsqueeze(1).to_broadcast([P, copies, cols]), ACT.Silu,
                      bias=vecs[:, V_CBT + f:V_CBT + f + 1], scale=vecs[:, V_CG + f:V_CG + f + 1]).then_inc(s_silu, 1)

            def conv_out(gang, f):
                for n in gang:
                    b, free = filled(act, ("cv", n, f))
                    A(y_cols(n)[:, f, 0, :], b[:, 0:width(n)], ACT.Identity, bias=vecs[:, V_DB + f:V_DB + f + 1]).then_inc(free, 1)

            even_in(GANGS[0])
            even_mixer(2)
            root(0, 2)
            front(0, 2)
            exps(0, 2)
            even_mixer(0)
            gelus(0, 2)
            root(0, 0)
            front(0, 0)
            exps(0, 0)
            even_in(GANGS[1])
            even_mixer(1)
            root(0, 1)
            front(0, 1)
            gelus(0, 0)
            exps(0, 1)
            root(1, 2)
            root(1, 0)
            odd_mixer(GANGS[0], {("conv", 3): lambda: gelus(0, 1)})
            conv_norm(2)
            conv_norm(0)
            root(2, 2)
            root(2, 0)
            queries(1, GANGS[0])
            scores(1, 2)
            exps(1, 2)
            scores(1, 0)
            root(1, 1)
            odd_mixer(GANGS[1], {("glu", 5): lambda: gelus(1, 2), ("glu", 7): lambda: exps(1, 0)})
            conv_norm(1)
            root(2, 1)
            front(1, 1)
            gelus(1, 0)
            exps(1, 1)
            root(3, 2)
            root(3, 0)
            gelus(1, 1)
            root(3, 1)

        @block.vector
        def _(dve):
            V = nc.vector
            count = {}

            def step(ins, s=s_dv):
                count[s.name] = count.get(s.name, 0) + 1
                ins.then_inc(s, 1)
                dve.wait_ge(s, count[s.name])

            used = [0]

            def use_row(tab, n, k, col):
                if tab == "u":
                    V.scalar_tensor_tensor(acc[:, k % 2, :], ring[:, k, :], 1.0, x[:, n, :], ALU.mult, ALU.mult,
                                           accum_out=actv[:, n, col]).then_inc(s_used, 1)
                else:
                    V.scalar_tensor_tensor(acc[:, k % 2, :], ring[:, k, :], actv[:, n, col], acc[:, k % 2, :],
                                           ALU.mult, ALU.add).then_inc(s_used, 1)

            def phase_of(at):
                return next(p for p in PHASES if p[4] <= at < p[4] + p[3])

            def enter(at):
                layer, tab, n, slots, start = phase_of(at)
                if tab == "v" and at == start:
                    step(V.memset(acc[:], 0.0))

            def leave(at):
                layer, tab, n, slots, start = phase_of(at - 1)
                if at != start + slots:
                    return
                dve.wait_ge(s_used, RING + at)
                if tab == "u":
                    k = [(l, m) for l, t, m, _, _ in PHASES if t == "u"].index((layer, n))
                    dve.sem_inc(s_act, 1)
                    dve.wait_ge(s_gel, k + 1)
                    step(V.tensor_tensor(actv[:, n, 0:slots], acg[:, 0:slots],
                                         gate[:, n].rearrange("p h k -> p (h k)")[:, 0:slots], ALU.mult))
                elif n == 2:
                    step(V.tensor_tensor(facc[:], acc[:, 0, :], acc[:, 1, :], ALU.add), s_facc)
                else:
                    step(V.scalar_tensor_tensor(x[:, n, :], x[:, n, :], ALPHA, acc[:, 0, :], ALU.mult, ALU.add))
                    step(V.tensor_tensor(x[:, n, :], x[:, n, :], acc[:, 1, :], ALU.add))

            def rows(batches=1):
                for _ in range(batches):
                    at = used[0]
                    enter(at)
                    _, tab, n, _, start = phase_of(at)
                    for k in range(RING):
                        dve.wait_ge(s_g[k], 16 * (at // RING + 1))
                        dve.wait_ge(s_used, RING + at + k - 1)
                        col = at - start + k
                        use_row(tab, n, k, slice(col, col + 1))
                    used[0] += RING
                    leave(used[0])

            def finish(phase):
                at = used[0]
                _, tab, n, slots, start = phase_of(at)
                end = start + slots
                assert PHASES[[p[:3] for p in PHASES].index(phase)] == phase_of(at)
                enter(at)
                with dve.Fori(0, (end - at) // RING) as i:
                    for k in range(RING):
                        dve.wait_ge(s_g[k], i * 16 + (at // RING + 1) * 16)
                        dve.wait_ge(s_used, i * RING + (RING + at + k - 1))
                        use_row(tab, n, k, bass.ds(i * RING + (at - start + k), 1))
                used[0] = end
                leave(end)

            def every(k, some):
                calls = [0]

                def seldom(batches=1):
                    calls[0] += 1
                    if calls[0] % k == 0:
                        some(batches)
                return seldom

            def nothing(batches=1):
                pass

            def inverse(root, var, r, t):
                step(V.reciprocal(r, root))
                step(V.tensor_tensor(t, r, r, ALU.mult))
                step(V.tensor_tensor(t, t, var, ALU.mult))
                step(V.tensor_scalar(t, t, -0.5, 1.5, ALU.mult, ALU.add))
                step(V.tensor_tensor(r, r, t, ALU.mult))

            def layer_norm(i, n, between=nothing):
                layer = i // 2
                dve.wait_ge(s_ln[i % 2], 32 * (i // 2 + 1))
                if i % 2 == 0:
                    pieces = [(("o", layer, n, blk), WC) for blk in range(D // WC)]
                elif n == 2:
                    pieces = [(("fold", layer, h), 512) for h in range(2)]
                else:
                    pieces = []
                for k, (name, w) in enumerate(pieces):
                    b, free = filled(dve, name)
                    xs = x[:, n, k * w:(k + 1) * w]
                    V.scalar_tensor_tensor(xs, xs, ALPHA, b[:, 0:w], ALU.mult, ALU.add).then_inc(free, 1)
                for name, _ in pieces:
                    moved(dve, name)
                for h in range(2):
                    last = V.bn_stats(bn[:, h, :], x[:, n, h * 512:(h + 1) * 512])
                    step(last)
                step(V.bn_aggr(mv[:, n, 0:2], bn[:].rearrange("p h c -> p (h c)")))
                step(V.tensor_scalar(mv[:, n, 2:3], mv[:, n, 1:2], EPS, None, ALU.add), s_var)
                between()
                dve.wait_ge(s_sd, NORMS.index((i, n)) + 1)
                inverse(mv[:, n, 3:4], mv[:, n, 2:3], mv[:, n, 4:5], mv[:, n, 5:6])
                step(V.tensor_scalar(x[:, n, :], x[:, n, :], mv[:, n, 0:1], mv[:, n, 4:5], ALU.subtract, ALU.mult))
                step(V.tensor_tensor(x[:, n, :], x[:, n, :], lnp[:, i % 2, 0, :], ALU.mult))
                step(V.tensor_tensor(x[:, n, :], x[:, n, :], lnp[:, i % 2, 1, :], ALU.add), s_xn)

            def top16(rows_, width_):
                aside = [spare[:, i, 0:width_] for i in range(len(rows_))]

                def await_all():
                    dve.wait_ge(s_dv, count[s_dv.name])

                def signal(ins):
                    count[s_dv.name] += 1
                    ins.then_inc(s_dv, 1)

                for vals, idx, src in rows_:
                    signal(V.max(vals[:, 0:8], src))
                await_all()
                for (vals, idx, src), left in zip(rows_, aside):
                    signal(V.match_replace(left, vals[:, 0:8], src, -3.0e38))
                    signal(V.max_index(idx[:, 0:8], vals[:, 0:8], src))
                await_all()
                for (vals, idx, src), left in zip(rows_, aside):
                    signal(V.max(vals[:, 8:16], left))
                await_all()
                for (vals, idx, src), left in zip(rows_, aside):
                    signal(V.max_index(idx[:, 8:16], vals[:, 8:16], left))
                await_all()

            def choose(layer, n, between=nothing):
                heads = HEADS_OF[n]
                c = CHOICES.index((layer, n))
                for f in range(0, 2 * heads, ABREAST):
                    moved(dve, ("s", layer, n, f // 4))
                    top16([(tv[:, i, :], ti[:, i, :], sc[:, i, :]) for i in range(f, f + ABREAST)], NK)
                    between()
                dve.sem_inc(s_sel, 1)
                g = 2 * heads
                step(V.tensor_copy(tif[:, 0:g, :], ti[:, 0:g, :]))
                for a0, a1, nb, c0 in ((0, A1, TOPK, 0), (A1, TOPK, B2, A1 * TOPK)):
                    na = a1 - a0
                    v1 = tv[:, 0:g:2, a0:a1].unsqueeze(3).to_broadcast([P, heads, na, nb])
                    v2 = tv[:, 1:g:2, 0:nb].unsqueeze(2).to_broadcast([P, heads, na, nb])
                    step(V.tensor_tensor(cand[:, 0:heads, c0:c0 + na * nb].rearrange("p h (a b) -> p h a b", a=na), v1, v2, ALU.add))
                between()
                for h in range(0, heads, ABREAST):
                    top16([(sv[:, i, :], ci[:, i, :], cand[:, i, :]) for i in range(h, h + ABREAST)], PAIRS)
                    between()
                step(V.tensor_tensor(gate[:, n, 0:heads, :], sv[:, 0:heads, :],
                                     sv[:, 0:heads, 0:1].to_broadcast([P, heads, TOPK]), ALU.subtract), s_sub)
                far = beyond[:, 0:heads, :]
                step(V.tensor_copy(far, ci[:, 0:heads, :]))
                step(V.tensor_scalar(far, far, float(A1 * TOPK), None, ALU.is_ge))
                for a, near_op, near_by, far_op, far_by, off in ((0, ALU.logical_shift_right, 4, ALU.logical_shift_right, 2, -12.0),
                                                                 (1, ALU.bitwise_and, 15, ALU.bitwise_and, 3, 0.0)):
                    step(V.tensor_single_scalar(cab[:, 0, 0:heads, :], ci[:, 0:heads, :], near_by, near_op))
                    step(V.tensor_single_scalar(cab[:, 1, 0:heads, :], ci[:, 0:heads, :], far_by, far_op))
                    step(V.tensor_copy(cabf[:, :, 0:heads, :], cab[:, :, 0:heads, :]))
                    near, other = cabf[:, 0, 0:heads, :], cabf[:, 1, 0:heads, :]
                    step(V.scalar_tensor_tensor(other, other, off, near, ALU.add, ALU.subtract))
                    step(V.tensor_tensor(other, other, far, ALU.mult))
                    step(V.tensor_tensor(near, near, other, ALU.add))
                    o = oh[:, 0:heads]
                    step(V.tensor_tensor(o, near.unsqueeze(3).to_broadcast([P, heads, TOPK, TOPK]),
                                         iota_f[:].unsqueeze(1).unsqueeze(1).to_broadcast([P, heads, TOPK, TOPK]),
                                         ALU.is_equal))
                    between()
                    step(V.tensor_tensor(o, o, tif[:, a:g:2, :].unsqueeze(2).to_broadcast([P, heads, TOPK, TOPK]), ALU.mult))
                    between()
                    step(V.tensor_reduce(key_no[:, a, 0:heads, :], o, AX.X, ALU.add))
                    between()
                step(V.tensor_scalar(key_no[:, 0, 0:heads, :], key_no[:, 0, 0:heads, :], float(NK), float(layer * NE),
                                     ALU.mult, ALU.add))
                step(V.tensor_tensor(eidx[:, n, 0:heads * TOPK].rearrange("p (h k) -> p h k", h=heads),
                                     key_no[:, 0, 0:heads, :], key_no[:, 1, 0:heads, :], ALU.add), s_e)
                dve.wait_ge(s_ex, c + 1)
                step(V.tensor_reduce(gsm[:, 0:heads], gate[:, n, 0:heads, :], AX.X, ALU.add))
                step(V.reciprocal(gsm[:, 0:heads], gsm[:, 0:heads]))
                step(V.tensor_tensor(gate[:, n, 0:heads, :], gate[:, n, 0:heads, :],
                                     gsm[:, 0:heads].unsqueeze(2).to_broadcast([P, heads, TOPK]), ALU.mult))

            def even_mixer(n, between=nothing):
                if n == 2:
                    moved(dve, ("stp",))
                dve.wait_ge(s_bz, 4)
                for j in range(JR):
                    moved(dve, ("z0", GANG[n], j))
                end = PB + (DS if n == 2 else P)
                src = ps_[:] if n == 2 else pp[:, :, n * P:PB + (n + 1) * P]
                tok = [pool_x[n](j)[..., PB:] for j in range(JR)]
                for lev in range(JR):
                    d, lo = 1 << lev, (2 << lev) - 1
                    dst = wab[:, lev % 2, :, 0:(DB if n == 2 else 1) * end]
                    if n == 2:
                        dst = dst.rearrange("p j (b t) -> p j b t", b=DB)
                    step(V.tensor_tensor(dst[:, lev:, ..., lo:end], src[:, lev:, ..., lo:end], src[:, lev:, ..., lo - d:end - d],
                                         ALU.add))
                    src = dst
                    out = in_sequences(n, y_cols(n)[:, lev, 0, :])
                    first = 0
                    if n == 0:
                        first = 16
                        step(V.tensor_tensor(out[:, 0:first], src[:, lev, PB:PB + first], inv_cnt[:, lev, :], ALU.mult))
                        step(V.tensor_tensor(out[:, 0:first], out[:, 0:first], tok[lev][:, 0:first], ALU.subtract))
                    V.scalar_tensor_tensor(out[..., first:], src[:, lev, ..., PB + first:end], 1.0 / (2 << lev), tok[lev][..., first:],
                                           ALU.mult, ALU.subtract).then_inc(s_pooled, 1)
                    if lev % 2:
                        between()
                buf = gates_x[n]
                if n == 2:
                    moved(dve, ("srh",))
                moved(dve, ("z0", GANG[n], 4 + JR - 1))
                rows_ = DS if n == 2 else P
                for w in range(4):
                    for j in range(JR):
                        tap = vecs[:, V_CW + 4 * w + j:V_CW + 4 * w + j + 1]
                        dst, src = in_sequences(n, buf[0][:, j, :]), conv_x[n](j)
                        if w == 0:
                            last = V.tensor_scalar(dst, src[..., 0:rows_], tap, vecs[:, V_CB + j:V_CB + j + 1], ALU.mult, ALU.add)
                        else:
                            last = V.scalar_tensor_tensor(dst, src[..., w:w + rows_], tap, dst, ALU.mult, ALU.add)
                        last.then_inc(s_xc if w == 3 else s_dv, 1)
                    if w < 3:
                        count[s_dv.name] += JR
                        dve.wait_ge(s_dv, count[s_dv.name])
                dve.wait_ge(s_xc, JR * (ORD[n] + 1))
                between()
                xc, rg, ig, th, uv, av = buf
                dve.wait_ge(s_th, JR * (ORD[n] + 1))
                step(V.tensor_scalar(uv, th, 1.0, None, ALU.add))
                step(V.reciprocal(uv, uv))
                step(V.scalar_tensor_tensor(th, th, 2.0, uv, ALU.mult, ALU.mult))
                step(V.tensor_scalar(av, th, -1.0, 1.0, ALU.mult, ALU.add))
                step(V.tensor_scalar(uv, th, -1.0, 2.0, ALU.mult, ALU.add))
                step(V.tensor_tensor(rg, th, uv, ALU.mult), s_q2)
                step(V.tensor_tensor(ig, ig, xc, ALU.mult))
                dve.wait_ge(s_rt, ORD[n] + 1)
                step(V.tensor_tensor(uv, th, ig, ALU.mult))
                if n == 2:
                    ap, up = [t.rearrange("p j (b s) -> p j b s", b=DB)[:, :, :, 0] for t in (av, uv)]
                    step(V.tensor_tensor(h0[:], h0[:], ap, ALU.mult))
                    step(V.tensor_tensor(up, up, h0[:], ALU.add))
                    step(V.memset(ap, 0.0))
                elif n == 1:
                    step(V.tensor_tensor(hlast_p[:], hlast_p[:], av[:, :, 0], ALU.mult))
                    step(V.tensor_tensor(uv[:, :, 0], uv[:, :, 0], hlast_p[:], ALU.add))
                for j in range(JR):
                    step(V.tensor_tensor_scan(xc[:, j, :], av[:, j, :], uv[:, j, :], 0.0, ALU.mult, ALU.add))
                if n == 2:
                    step(V.tensor_copy(hlast_s[:], xc[:, :, DS - 1:NS:DS]))
                else:
                    step(V.tensor_copy(hlast_p[:], xc[:, :, P - 1]))
                moved(dve, ("z0", GANG[n], 11))
                y = y_cols(n)[:, JR:]
                if n == 2:
                    step(V.tensor_tensor(y[:, :, 1, :], xc, y[:, :, 0, :], ALU.mult))
                    step(V.tensor_copy(y[:, :, 0, :], y[:, :, 1, :]), s_yb)
                else:
                    step(V.tensor_tensor(y[:, :, 0, :], xc, y[:, :, 0, :], ALU.mult), s_yb)
                between()

            def glu_steps(gang):
                for f in range(KD):
                    k = KD * GANGS.index(gang) + f
                    if f == 0:
                        dve.wait_ge(s_hist, 1)
                    b, free = filled(dve, ("z1", gang, f))
                    dve.wait_ge(s_sig, k + 1)
                    for n in gang:
                        at = COL[n] - COL[gang[0]]
                        val, gt = [in_sequences(n, t[:, at:at + width(n)]) for t in (b, sg[:, k % 2, :])]
                        last = V.tensor_tensor(glu_x[n](f)[..., CB:], val, gt, ALU.mult)
                    last.then_inc(free, 1)
                    moved(dve, ("z1", gang, f))
                    dve.sem_inc(s_glu, 1)
                    yield f

            def glu(gang, between):
                for _ in glu_steps(gang):
                    between()

            def conv_norm(n, between):
                cols = width(n)
                y = y_cols(n)[:, :, 0, :]
                moved(dve, ("mu", n))
                step(V.tensor_tensor(y, y, mub[:, 0:cols].unsqueeze(1).to_broadcast([P, KD, cols]), ALU.subtract), s_cm)
                b, free = filled(dve, ("var", n))
                V.tensor_scalar(rsb[:, 0, 0:cols], b[:, 0:cols], EPS, None, ALU.add).then_inc(free, 1)
                moved(dve, ("var", n))
                dve.sem_inc(s_cve, 1)
                dve.wait_ge(s_csd, ORD[n] + 1)
                r = [rsb[:, i, 0:cols] for i in range(3)]
                inverse(r[1], r[0], r[2], mub[:, 0:cols])
                step(V.tensor_tensor(sq[:, 0:KD * cols].rearrange("p (f t) -> p f t", f=KD), y,
                                     r[2].unsqueeze(1).to_broadcast([P, KD, cols]), ALU.mult), s_cn)
                between()

            dve.sem_inc(s_used, RING)
            dve.wait_ge(s_cst, 6)
            step(V.tensor_copy(iota_f[:], iota_i[:]))
            for j in range(JR):
                step(V.tensor_scalar(inv_cnt[:, j, :], iota_f[:], 1.0, float(2 << j), ALU.add, ALU.min))
            step(V.reciprocal(inv_cnt[:], inv_cnt[:]))
            moved(dve, ("vec",))
            lam = vecs[:, V_LAM:V_LAM + JR]
            step(V.tensor_scalar(sm[:, 8:12], lam, -1.0, None, ALU.mult))
            step(V.tensor_tensor(sm[:, 0:4], sm[:, 8:12], lam, ALU.min), s_lam1)
            dve.wait_ge(s_lam2, 1)
            e, z, s2, p = sm[:, 4:8], sm[:, 12:16], sm[:, 16:20], sm[:, 20:24]
            step(V.tensor_scalar(z, e, 2.0, None, ALU.add))
            step(V.reciprocal(z, z))
            step(V.tensor_tensor(z, z, e, ALU.mult))
            step(V.tensor_tensor(s2, z, z, ALU.mult))
            step(V.tensor_scalar(p, s2, 1.0 / 17, None, ALU.mult))
            for c in (15, 13, 11, 9, 7, 5, 3):
                step(V.scalar_tensor_tensor(p, p, 1.0 / c, s2, ALU.add, ALU.mult))
            step(V.scalar_tensor_tensor(p, p, 1.0, z, ALU.add, ALU.mult))
            step(V.tensor_scalar(sm[:, 8:12], sm[:, 8:12], 0.0, 4.0, ALU.max, ALU.mult))
            step(V.scalar_tensor_tensor(spc[:], p, 8.0, sm[:, 8:12], ALU.mult, ALU.add), s_spc)

            even_mixer(2)
            layer_norm(0, 2)
            choose(0, 2)
            rows(2)
            even_mixer(0, rows)
            rows(2)
            layer_norm(0, 0, rows)
            rows(3)
            choose(0, 0, every(4, rows))
            finish((0, "v", 2))
            rows(2)
            even_mixer(1, rows)
            rows(2)
            layer_norm(0, 1, rows)
            rows(5)
            choose(0, 1, rows)
            layer_norm(1, 2, rows)
            finish((0, "v", 0))
            layer_norm(1, 0, rows)
            rows(3)
            glu(GANGS[0], rows)
            rows(10)
            conv_norm(2, rows)
            conv_norm(0, nothing)
            rows(2)
            layer_norm(2, 2, rows)
            layer_norm(2, 0)
            rows(4)
            choose(1, 2, every(6, rows))
            finish((0, "v", 1))
            layer_norm(1, 1, rows)
            rows(2)
            steps = glu_steps(GANGS[1])
            seldom = every(2, rows)

            def glu_and_rows():
                if next(steps, None) is None:
                    seldom()
                else:
                    rows()

            choose(1, 0, glu_and_rows)
            finish((1, "v", 2))
            rows(1)
            conv_norm(1, rows)
            rows(2)
            layer_norm(2, 1, rows)
            rows(5)
            choose(1, 1, rows)
            layer_norm(3, 2, rows)
            finish((1, "v", 0))
            layer_norm(3, 0, rows)
            finish((1, "u", 1))
            finish((1, "v", 1))
            layer_norm(3, 1)
            assert used[0] == ROWS

        @block.gpsimd
        def _(pool):
            G = nc.gpsimd
            G.memset(ident[:], 0.0).then_inc(s_cst, 1)
            G.memset(foldm[:], 0.0).then_inc(s_cst, 1)
            G.memset(mean_m[:], 1.0 / D).then_inc(s_cst, 1)
            pool.wait_ge(s_cst, 2)
            G.affine_select(out=ident[:], in_=ident[:], compare_op=ALU.not_equal, fill=1.0, base=0,
                            pattern=[[-1, P]], channel_multiplier=1).then_inc(s_cst, 1)
            f = foldm[:].rearrange("p (h q) -> p h q", h=2)
            G.affine_select(out=f, in_=f, compare_op=ALU.not_equal, fill=1.0, base=0,
                            pattern=[[0, 2], [-1, NS]], channel_multiplier=1).then_inc(s_cst, 1)
            pool.wait_ge(s_cst, 5)
            G.iota(iota_i[:], pattern=[[1, 16]], base=0, channel_multiplier=0).then_inc(s_cst, 1)
            G.affine_select(out=f, in_=f, compare_op=ALU.not_equal, fill=1.0, base=-NS,
                            pattern=[[0, 2], [-1, NS]], channel_multiplier=1).then_inc(s_cst, 1)
            G.memset(bda[:], 0.0).then_inc(s_bz, 1)
            G.memset(bdx[:], 0.0).then_inc(s_bz, 1)
            G.memset(pp[:, :, 0:PB], 0.0).then_inc(s_bz, 1)
            G.memset(rp[:, :, 0:RB], 0.0).then_inc(s_bz, 1)

            tables = {"u": peer_u.rearrange("l e d -> (l e) d"), "v": peer_v.rearrange("l e d -> (l e) d")}
            for layer, tab, n, slots, start in PHASES:
                if (layer, tab, n) == (0, "u", 1):
                    pool.wait_ge(s_xn, NORMS.index((0, 1)) + 1)
                    G.memset(cp[:, :, 0:CB], 0.0).then_inc(s_hist, 1)
                pool.wait_ge(s_e, CHOICES.index((layer, n)) + 1)
                with pool.Fori(0, slots // (2 * RING)) as i:
                    for h in range(2):
                        G.tensor_copy(stg[:, h, :], eidx[:, n, bass.ds(i * 2 * RING + h * RING, RING)]).then_inc(s_stg, 1)
                        pool.wait_ge(s_stg, i * 2 + (start // RING + h + 1))
                        for k in range(RING):
                            pool.wait_ge(s_used, i * 2 * RING + (start + h * RING + k + 1))
                            pool.sem_inc(s_turn, 1)
                            G.indirect_dma_start(ring[:, k, :], None, tables[tab],
                                                 bass.IndirectOffsetOnAxis(stg[:, h, k:k + 1], 0)).then_inc(s_g[k], 16)


_INS = ['x_prompt', 'x_sample', 'state_pool', 'state_rnn_conv', 'state_rnn_h', 'state_conv',
        'w_in_even', 'pool_w', 'pool_scale', 'rnn_conv_w', 'rnn_conv_b', 'rg_wa', 'rg_ba', 'rg_wx', 'rg_bx',
        'rg_lambda', 'w_out_even', 'w_glu', 'dw_w', 'dw_b', 'conv_ln_g', 'conv_ln_b', 'w_pw',
        'peer_wq', 'peer_k1', 'peer_k2', 'peer_u', 'peer_v', 'ln_mix_g', 'ln_mix_b', 'ln_ffn_g', 'ln_ffn_b']
_OUTS = [(1, SEQ, D), (DB, DS, D), (1, 1, PB, HALF), (1, 1, RB, HALF), (1, 1, HALF), (1, 1, CB, D),
         (1, DB, PB, HALF), (1, DB, RB, HALF), (1, DB, HALF), (1, DB, CB, D)]


def kernel(**inputs):
    import numpy as _np
    import concourse.bacc as _bacc
    from concourse import mybir as _mybir
    from concourse.bass_utils import run_bass_kernel_spmd as _run

    nc = _bacc.Bacc("TRN2", target_bir_lowering=False, num_devices=1)
    arrays, args = {}, []
    for name in _INS:
        a = _np.ascontiguousarray(inputs[name])
        arrays[f"in_{name}_dram"] = a
        args.append(nc.dram_tensor(f"in_{name}_dram", a.shape, _mybir.dt.from_np(a.dtype), kind="ExternalInput").ap())
    for i, shape in enumerate(_OUTS):
        args.append(nc.dram_tensor(f"out_{i}_dram", shape, _mybir.dt.float32, kind="ExternalOutput").ap())
    build(nc, *args)
    r = _run(nc, [arrays], core_ids=[0])
    return tuple(r.results[0][f"out_{i}_dram"] for i in range(len(_OUTS)))
```
